# Optimizing a Trainium2 kernel written in Bass

```python
import math
import jax, jax.numpy as jnp
from jax import lax
import numpy as np

D_MODEL = 1024
BATCH = 1
SEQ = 512
DEPTH = 1

HEAD_DIM = 64
A_HEADS = 4
A_VDIM = 2 * HEAD_DIM
B_HEADS = 8
B_KV_HEADS = 2
B_GROUP = B_HEADS // B_KV_HEADS
A_OUT = A_HEADS * A_VDIM
B_OUT = B_HEADS * HEAD_DIM
D_MIX = A_OUT + B_OUT
A_QK = A_HEADS * 2 * HEAD_DIM
B_Q = B_HEADS * HEAD_DIM
B_KV = B_KV_HEADS * HEAD_DIM
SPLITS = (A_QK, A_QK, A_OUT, B_Q, B_KV, B_KV)
D_IN_PROJ = sum(SPLITS)
Q_BLOCK = 128
GRID_W = 64
ROPE_THETA = 10000.0
EPS = 1e-6
N_EXPERTS = 32
TOP_K = 4
D_EXPERT = 1024
SWIGLU_LIMIT = 7.0
SWIGLU_ALPHA = 1.702
MOE_BLOCK = 256

kernel_name = "hymba_diffattn_axialgqa_moe_encoder"

def lambda_init(layer):
    return 0.8 - 0.6 * math.exp(-0.3 * layer)

def rms_norm(x, g):
    xf = x.astype(jnp.float32)
    y = xf * lax.rsqrt(jnp.mean(xf * xf, axis=-1, keepdims=True) + EPS)
    return (y * g.astype(jnp.float32)).astype(x.dtype)

def rope_freqs(dim):
    return ROPE_THETA ** (-(jnp.arange(0, dim, 2, dtype=jnp.float32) / dim))

def apply_rope(x, ang):
    cos = jnp.cos(ang).astype(x.dtype)
    sin = jnp.sin(ang).astype(x.dtype)
    x1, x2 = jnp.split(x, 2, axis=-1)
    return jnp.concatenate([x1 * cos - x2 * sin, x2 * cos + x1 * sin], axis=-1)

def to_blocks(t):
    s, d = t.shape[-2], t.shape[-1]
    t = t.reshape(*t.shape[:-2], s // Q_BLOCK, Q_BLOCK, d)
    return jnp.moveaxis(t, -3, 0)

def from_blocks(o):
    o = jnp.moveaxis(o, 0, -3)
    return o.reshape(*o.shape[:-3], o.shape[-3] * o.shape[-2], o.shape[-1])

def diff_attention(q1, q2, k1, k2, v, lam):
    scale = HEAD_DIM ** -0.5

    def block(qs):
        qb1, qb2 = qs
        s1 = jnp.einsum('bhqd,bhkd->bhqk', qb1, k1).astype(jnp.float32) * scale
        s2 = jnp.einsum('bhqd,bhkd->bhqk', qb2, k2).astype(jnp.float32) * scale
        p = jax.nn.softmax(s1, axis=-1) - lam * jax.nn.softmax(s2, axis=-1)
        return jnp.einsum('bhqk,bhkd->bhqd', p.astype(v.dtype), v)

    return from_blocks(lax.map(block, (to_blocks(q1), to_blocks(q2))))

def gqa_attention(q, k, v):
    scale = HEAD_DIM ** -0.5

    def block(qb):
        s = jnp.einsum('bgrqd,bgkd->bgrqk', qb, k).astype(jnp.float32) * scale
        p = jax.nn.softmax(s, axis=-1)
        return jnp.einsum('bgrqk,bgkd->bgrqd', p.astype(v.dtype), v)

    return from_blocks(lax.map(block, to_blocks(q)))

def moe_ffn(h, router_w, router_b, w_gate, b_gate, w_up, b_up, w_down, b_down):
    b, s, d = h.shape
    n = b * s
    xf = h.reshape(n, d)
    logits = xf.astype(jnp.float32) @ router_w.astype(jnp.float32) + router_b.astype(jnp.float32)
    top_vals, top_idx = lax.top_k(logits, TOP_K)
    gates = jax.nn.softmax(top_vals, axis=-1)
    nk = n * TOP_K
    expert_flat = top_idx.reshape(nk)
    gates_flat = gates.reshape(nk)
    token_of = jnp.arange(nk, dtype=jnp.int32) // TOP_K
    order = jnp.argsort(expert_flat)
    sorted_e = expert_flat[order]
    counts = jnp.zeros((N_EXPERTS,), jnp.int32).at[expert_flat].add(1)
    offsets = jnp.cumsum(counts) - counts
    padded = ((counts + MOE_BLOCK - 1) // MOE_BLOCK) * MOE_BLOCK
    pad_end = jnp.cumsum(padded)
    pad_start = pad_end - padded
    rank = jnp.arange(nk, dtype=jnp.int32) - offsets[sorted_e]
    dest = pad_start[sorted_e] + rank
    n_slots = nk + N_EXPERTS * MOE_BLOCK
    n_blocks = n_slots // MOE_BLOCK
    slot_token = jnp.full((n_slots,), n, jnp.int32).at[dest].set(token_of[order])
    slot_gate = jnp.zeros((n_slots,), jnp.float32).at[dest].set(gates_flat[order])
    block_start = jnp.arange(n_blocks, dtype=jnp.int32) * MOE_BLOCK
    block_expert = jnp.clip(jnp.searchsorted(pad_end, block_start, side='right'), 0, N_EXPERTS - 1)
    xpad = jnp.concatenate([xf, jnp.zeros((1, d), xf.dtype)], axis=0)
    xs = xpad[slot_token].reshape(n_blocks, MOE_BLOCK, d)

    def expert_block(args):
        xb, e = args
        g = xb @ w_gate[e] + b_gate[e]
        u = xb @ w_up[e] + b_up[e]
        g = jnp.minimum(g, SWIGLU_LIMIT)
        u = jnp.clip(u, -SWIGLU_LIMIT, SWIGLU_LIMIT)
        mid = (u + 1.0) * (g * jax.nn.sigmoid(SWIGLU_ALPHA * g))
        return mid @ w_down[e] + b_down[e]

    ys = lax.map(expert_block, (xs, block_expert)).reshape(n_slots, d)
    out = jnp.zeros((n + 1, d), ys.dtype).at[slot_token].add(ys * slot_gate[:, None].astype(ys.dtype))
    return out[:n].reshape(b, s, d)

def setup_inputs(seed: int = 0) -> dict:
    key = jax.random.key(seed)
    ks = jax.random.split(key, 24)
    f = jnp.float32

    def nrm(k, shape, scale):
        return jax.random.normal(k, shape, f) * scale

    def gain(k, shape):
        return 1.0 + 0.02 * jax.random.normal(k, shape, f)

    L = DEPTH
    return {
        "x": jax.random.normal(ks[0], (BATCH, SEQ, D_MODEL), f),
        "norm1_g": gain(ks[1], (L, D_MODEL)),
        "w_in": nrm(ks[2], (L, D_MODEL, D_IN_PROJ), D_MODEL ** -0.5),
        "a_qnorm_g": gain(ks[3], (L, HEAD_DIM)),
        "a_knorm_g": gain(ks[4], (L, HEAD_DIM)),
        "a_lq1": nrm(ks[5], (L, HEAD_DIM), 0.1),
        "a_lk1": nrm(ks[6], (L, HEAD_DIM), 0.1),
        "a_lq2": nrm(ks[7], (L, HEAD_DIM), 0.1),
        "a_lk2": nrm(ks[8], (L, HEAD_DIM), 0.1),
        "a_subln_g": gain(ks[9], (L, A_VDIM)),
        "b_qnorm_g": gain(ks[10], (L, HEAD_DIM)),
        "b_knorm_g": gain(ks[11], (L, HEAD_DIM)),
        "w_out": nrm(ks[12], (L, D_MIX, D_MODEL), D_MIX ** -0.5),
        "norm2_g": gain(ks[13], (L, D_MODEL)),
        "router_w": nrm(ks[14], (L, D_MODEL, N_EXPERTS), D_MODEL ** -0.5),
        "router_b": nrm(ks[15], (L, N_EXPERTS), 0.01),
        "w_gate": nrm(ks[16], (L, N_EXPERTS, D_MODEL, D_EXPERT), D_MODEL ** -0.5),
        "b_gate": nrm(ks[17], (L, N_EXPERTS, D_EXPERT), 0.01),
        "w_up": nrm(ks[18], (L, N_EXPERTS, D_MODEL, D_EXPERT), D_MODEL ** -0.5),
        "b_up": nrm(ks[19], (L, N_EXPERTS, D_EXPERT), 0.01),
        "w_down": nrm(ks[20], (L, N_EXPERTS, D_EXPERT, D_MODEL), D_EXPERT ** -0.5),
        "b_down": nrm(ks[21], (L, N_EXPERTS, D_MODEL), 0.01),
    }

def reference(x, norm1_g, w_in, a_qnorm_g, a_knorm_g, a_lq1, a_lk1, a_lq2, a_lk2,
              a_subln_g, b_qnorm_g, b_knorm_g, w_out, norm2_g, router_w, router_b,
              w_gate, b_gate, w_up, b_up, w_down, b_down):
    b, s, _ = x.shape
    rows = s // GRID_W
    t = jnp.arange(s, dtype=jnp.float32)
    ang_1d = t[:, None] * rope_freqs(HEAD_DIM)[None, :]
    row = jnp.repeat(jnp.arange(rows, dtype=jnp.float32), GRID_W)
    col = jnp.tile(jnp.arange(GRID_W, dtype=jnp.float32), rows)
    f_ax = rope_freqs(HEAD_DIM // 2)
    ang_2d = jnp.concatenate([row[:, None] * f_ax[None, :], col[:, None] * f_ax[None, :]], axis=-1)
    split_idx = list(np.cumsum(SPLITS)[:-1])

    for layer in range(DEPTH):
        lam_init = lambda_init(layer)
        h = rms_norm(x, norm1_g[layer])
        proj = h @ w_in[layer]
        qa, ka, va, qb, kb, vb = jnp.split(proj, split_idx, axis=-1)

        qa = qa.reshape(b, s, A_HEADS, 2, HEAD_DIM).transpose(3, 0, 2, 1, 4)
        ka = ka.reshape(b, s, A_HEADS, 2, HEAD_DIM).transpose(3, 0, 2, 1, 4)
        va = va.reshape(b, s, A_HEADS, A_VDIM).transpose(0, 2, 1, 3)
        qa = apply_rope(rms_norm(qa, a_qnorm_g[layer]), ang_1d)
        ka = apply_rope(rms_norm(ka, a_knorm_g[layer]), ang_1d)
        lam = (jnp.exp(jnp.sum(a_lq1[layer].astype(jnp.float32) * a_lk1[layer].astype(jnp.float32)))
               - jnp.exp(jnp.sum(a_lq2[layer].astype(jnp.float32) * a_lk2[layer].astype(jnp.float32)))
               + lam_init)
        oa = diff_attention(qa[0], qa[1], ka[0], ka[1], va, lam)
        oa = rms_norm(oa, a_subln_g[layer]) * (1.0 - lam_init)
        oa = oa.transpose(0, 2, 1, 3).reshape(b, s, A_OUT)

        qb = qb.reshape(b, s, B_HEADS, HEAD_DIM).transpose(0, 2, 1, 3)
        kb = kb.reshape(b, s, B_KV_HEADS, HEAD_DIM).transpose(0, 2, 1, 3)
        vb = vb.reshape(b, s, B_KV_HEADS, HEAD_DIM).transpose(0, 2, 1, 3)
        qb = apply_rope(rms_norm(qb, b_qnorm_g[layer]), ang_2d)
        kb = apply_rope(rms_norm(kb, b_knorm_g[layer]), ang_2d)
        qb = qb.reshape(b, B_KV_HEADS, B_GROUP, s, HEAD_DIM)
        ob = gqa_attention(qb, kb, vb)
        ob = ob.reshape(b, B_HEADS, s, HEAD_DIM).transpose(0, 2, 1, 3).reshape(b, s, B_OUT)

        x = x + jnp.concatenate([oa, ob], axis=-1) @ w_out[layer]

        h2 = rms_norm(x, norm2_g[layer])
        x = x + moe_ffn(h2, router_w[layer], router_b[layer], w_gate[layer], b_gate[layer],
                        w_up[layer], b_up[layer], w_down[layer], b_down[layer])
    return x


_drawn_inputs = setup_inputs


def setup_inputs(seed=0):
    import zlib

    import numpy as np

    out = dict(_drawn_inputs(seed))
    spreads = {}
    factors = {'a_lq1': 98.944,
     'b_qnorm_g': 8.0,
     'b_knorm_g': 6.511,
     'b_gate': 8.0,
     'b_up': 23.065,
     'b_down': 8.0,
     'a_knorm_g': 3.071,
     'router_b': 2.729}
    for name, (base, spread) in spreads.items():
        noise = np.random.default_rng([zlib.crc32(name.encode()), seed]).standard_normal(out[name].shape)
        drawn = base * np.exp(spread * noise) if base else spread * noise
        out[name] = __import__('jax').numpy.asarray(drawn.astype(out[name].dtype))
    for name, factor in factors.items():
        out[name] = (out[name] * factor).astype(out[name].dtype)
    return out
```

```python
from contextlib import ExitStack

import numpy as np

import concourse.bass as bass
from concourse import mybir

F32 = mybir.dt.float32
F32R = mybir.dt.float32r
I32 = mybir.dt.int32
U32 = mybir.dt.uint32
ALU = mybir.AluOpType
ACT = mybir.ActivationFunctionType
AX = mybir.AxisListType

P = 128
SEQ = 512
D = 1024
T = SEQ // P
C = D // P
HD = 64
NQK = 26
NCH = NQK // 2
VW = 640
WIN = 2304
PAIRS = 8
NU = T * PAIRS
EPS = 1e-6
LAM_INIT = 0.2
SCALE = HD ** -0.5

E = 32
TOPK = 4
SLOTS = 96
OVER = SEQ * TOPK // SLOTS
NB = E + OVER + 3
NX = NB - E
NTHR = (SEQ - 1) // SLOTS
FAR = 4096.0
LIMIT = 7.0
ALPHA = 1.702
HALF = D // 2
UNITS = 2 * C
RING = 4
ROWS = SEQ + SLOTS

K_ID, K_TRI, K_ONE, K_SLOT, K_BIDX, K_E32, K_THR, K_CUM, K_SPARE = (
    0, 128, 256, 384, 480, 480 + NX, 512 + NX, 520 + NX, 584 + NX)
K_HALF = K_SPARE + 1
K_W = K_HALF + 1
C_G1, C_G2, C_RW = 0, C, 2 * C
C_W = C_RW + C * E
V_GAIN, V_LAM, V_SUB = 0, 4 * HD, 8 * HD
V_W = V_SUB + 128


def shape_constants():
    k = np.zeros((P, K_W), np.float32)
    k[:, K_ID:K_ID + P] = np.eye(P)
    k[:, K_TRI:K_TRI + P] = np.triu(np.ones((P, P)), 1)
    k[:, K_ONE:K_ONE + P] = 1.0
    k[:, K_SLOT:K_SLOT + SLOTS] = np.arange(SLOTS) - FAR
    k[:, K_BIDX:K_BIDX + NX] = np.arange(NX)
    k[:, K_E32:K_E32 + E] = np.arange(E)
    k[:, K_THR:K_THR + NTHR] = SLOTS * np.arange(1, NTHR + 1)
    k[:E, K_CUM:K_CUM + E] = np.triu(np.ones((E, E)))
    k[:E, K_CUM + E:K_CUM + 2 * E] = np.eye(E)
    k[:, K_SPARE] = SEQ + np.arange(P)
    k[:, K_HALF] = -0.5

    def freqs(dim):
        return np.float32(10000.0) ** (-(np.arange(0, dim, 2, dtype=np.float32) / np.float32(dim)))

    t = np.arange(SEQ, dtype=np.float32)
    one = t[:, None] * freqs(HD)[None]
    f = freqs(HD // 2)
    two = np.concatenate([(np.arange(SEQ) // 64).astype(np.float32)[:, None] * f,
                          (np.arange(SEQ) % 64).astype(np.float32)[:, None] * f], -1)
    rope = np.zeros((SEQ, 4, HD), np.float32)
    for n, a in enumerate((one, two)):
        a = a.astype(np.float32)
        rope[:, 2 * n] = np.concatenate([np.cos(a), np.cos(a)], -1)
        rope[:, 2 * n + 1] = np.concatenate([np.sin(a), -np.sin(a)], -1)
    rope = rope.reshape(T, P, 4 * HD).transpose(1, 0, 2)
    slot = np.zeros((P, T, E, 3), np.float32)
    slot[..., 0] = (np.arange(T)[None, :] * P + np.arange(P)[:, None])[:, :, None]
    slot[..., 2] = 1.0
    return k, np.ascontiguousarray(rope), slot.reshape(P, T, E * 3)


def encoder_layer(nc, x, w_in, w_out, w_gate, w_up, w_down, b_down, router_b,
                  consts, rope_c, slot_c, cols_c, bias_c, vecs_c, out, h2_rows):
    with ExitStack() as ctx:
        def sb(name, shape, dt=F32):
            return ctx.enter_context(nc.sbuf_tensor(name, shape, dt))

        def sem(name):
            return ctx.enter_context(nc.semaphore(name))

        bank = [ctx.enter_context(nc.psum_tensor(f"bank{i}", [P, 512], F32)) for i in range(8)]

        W = sb("weights", [P, 3 * C * D])
        w_in_sb = W[:, 0:C * WIN].rearrange("p (c n) -> p c n", c=C)
        wg = W[:, 0:C * D].rearrange("p (c n) -> p c n", c=C)
        wu = W[:, C * D:2 * C * D].rearrange("p (c n) -> p c n", c=C)
        wd = W[:, 2 * C * D:3 * C * D].rearrange("p (c n) -> p c n", c=C)
        w_out_sb = wd

        xres = sb("xres", [P, T, D])
        region2 = sb("region2", [P, T * D])
        xT = region2[:, :].rearrange("p (c s) -> p c s", c=C)
        o_nat = region2[:, :].rearrange("p (t d) -> p t d", t=T)
        w_in_end = C * WIN
        qk = [sb("qk", [P, NQK * HD])[:, :], W[:, w_in_end:w_in_end + NQK * HD]]
        qk = [q.rearrange("p (n d) -> p n d", n=NQK) for q in qk]
        bd = W[0:E, 7 * D:8 * D]
        h2T = W[:, 8 * D:9 * D].rearrange("p (c s) -> p c s", c=C)
        oT = W[:, 9 * D:11 * D].rearrange("p (b c s) -> p b c s", b=2, c=C)
        GT = sb("GT", [E, P])
        region4 = sb("region4", [P, NCH * SEQ])
        qkT = region4[:, :].rearrange("p (n s) -> p n s", n=NCH)
        t1, t2 = (W[:, w_in_end + i * NQK * HD:w_in_end + (i + 1) * NQK * HD].rearrange("p (n d) -> p n d", n=NQK)
                  for i in (1, 2))
        xsq = W[:, w_in_end + NQK * HD:w_in_end + NQK * HD + D]
        rope = W[:, w_in_end + 3 * NQK * HD:w_in_end + 3 * NQK * HD + T * 4 * HD].rearrange("p (t n) -> p t n", t=T)
        prob = W[:, 11 * D:14 * D].rearrange("p (b m k) -> p b m k", b=3, m=2)
        probT = W[:, 14 * D:16 * D].rearrange("p (b m j q) -> p b m j q", b=2, m=2, j=4)
        CS = C * SLOTS
        gact, uact, sig, mid = (region2[:, i * CS:(i + 1) * CS].rearrange("p (c s) -> p c s", c=C) for i in range(4))
        xrow = region2[:, 4 * CS:4 * CS + D]
        taken = [0]

        def late(n, parts=P):
            taken[0] += n
            assert taken[0] <= NCH * SEQ
            return region4[0:parts, taken[0] - n:taken[0]]

        xu = late(CS).rearrange("p (c s) -> p c s", c=C)
        bias = late(2 * C * E)
        le = late(NX * E).rearrange("p (j e) -> p j e", j=NX)
        onehot = late(T * SLOTS).rearrange("p (t s) -> p t s", t=T)
        slot_b = late(SLOTS)
        nbc = late(P, E)
        cum = late(2 * E)
        tab_e = late(NB)
        tab_base = late(NB)
        gtab = late(NB, SLOTS)
        stab = late(NB, SLOTS)
        Rcur = late(3 * T).rearrange("p (t k) -> p t k", t=T)
        bgc, buc, cnt = late(C), late(C), late(16, E)
        btab = late(4 * NX).rearrange("p (k j) -> p k j", k=4)
        V = sb("V", [P, T, VW])
        v_flat = V[:, :, :].rearrange("p t n -> p (t n)")
        y_sb = v_flat[:, 0:D]
        xg = v_flat[:, D:D + CS].rearrange("p (c s) -> p c s", c=C)
        w_hi = sb("w_hi", [P, RING, HALF], F32R)
        w_lo = sb("w_lo", [P, RING, HALF], F32R)
        mid_hi = sb("mid_hi", [P, C, SLOTS], F32R)
        mid_lo = sb("mid_lo", [P, C, SLOTS], F32R)
        K = sb("K", [P, K_W])
        ropeg = sb("ropeg", [P, 8, HD])
        sq = ropeg[:, :, :].rearrange("p n d -> p (n d)")
        cols = sb("cols", [P, C_W])
        vecs = sb("vecs", [P, V_W])
        rb = sb("rb", [1, E])
        st = sb("st", [P, 64])
        ssq = sb("ssq", [P, NQK])
        rsq = sb("rsq", [P, NQK])
        mx = sb("mx", [P, 4, 2])
        nmx = sb("nmx", [P, 4, 2])
        rs = sb("rs", [P, 4, 2])
        rr = sb("rr", [P, 4, 2])
        nla = sb("nla", [P, 4])
        sub = sb("sub", [P, 8])
        subg = sb("subg", [P, 128])
        lg = sb("lg", [P, E])
        v8 = sb("v8", [P, 8])
        i8 = sb("i8", [P, 8], U32)
        i8f = sb("i8f", [P, 8])
        e4 = sb("e4", [P, 8])
        g4 = sb("g4", [P, 4])
        oh4 = sb("oh4", [P, 4, E])
        ohg = sb("ohg", [P, 4, E])
        M = sb("M", [P, T, E])
        R = sb("R", [P, T, E, 3])
        pos = sb("pos", [P, T, E])
        tab_ei = sb("tab_ei", [P, NB], I32)
        further = sb("further", [P, 1], I32)
        si = sb("si", [SLOTS, 4])
        gidx = sb("gidx", [SLOTS, 1], I32)
        sidx = sb("sidx", [SLOTS, 1], I32)
        gnow = sb("gnow", [SLOTS, 1])

        ident = K[:, K_ID:K_ID + P]
        gain = vecs[:, V_GAIN:V_GAIN + 4 * HD].rearrange("p (n d) -> p n d", n=4)
        lamv = vecs[:, V_LAM:V_LAM + 4 * HD].rearrange("p (n d) -> p n d", n=4)
        bgate = bias[:, 0:C * E].rearrange("p (c e) -> p c e", c=C)
        bup = bias[:, C * E:2 * C * E].rearrange("p (c e) -> p c e", c=C)
        rw = cols[:, C_RW:C_RW + C * E].rearrange("p (c e) -> p c e", c=C)

        x_in = [sem(f"x_in{t}") for t in range(T)]
        K_in, cols_in, const_in = sem("K_in"), sem("cols_in"), sem("const_in")
        win_in = [sem(f"win_in{c}") for c in range(C)]
        wout_in, bd_in, bias_in = sem("wout_in"), sem("bd_in"), sem("bias_in")
        wg_in = [sem(f"wg_in{j}") for j in range(C // 2)]
        wu_in = [sem(f"wu_in{j}") for j in range(C // 2)]
        wd_in = [sem(f"wd_in{j}") for j in range(C // 2)]
        dve_step = sem("dve_step")
        act_step = sem("act_step")
        lam_dot, lam_exp, lam_ready = sem("lam_dot"), sem("lam_exp"), sem("lam_ready")
        xss, mean_ready, root_ready = sem("xss"), sem("mean_ready"), sem("root_ready")
        xT_tr, xT_ready = sem("xT_tr"), sem("xT_ready")
        proj_done, proj_out = sem("proj_done"), sem("proj_out")
        qk_sq, qk_rope, qkT_tr, qkT_ready = sem("qk_sq"), sem("qk_rope"), sem("qkT_tr"), sem("qkT_ready")
        sc_done, max_ready, exp_done, comb_done, rcp_done = (
            sem("sc_done"), sem("max_ready"), sem("exp_done"), sem("comb_done"), sem("rcp_done"))
        pT_tr, pT_act, pT_dve, pv_done, oA_out, oB_out, o_ready = (
            sem("pT_tr"), sem("pT_act"), sem("pT_dve"), sem("pv_done"), sem("oA_out"), sem("oB_out"), sem("o_ready"))
        oT_tr, oT_ready, op_done, res_ready = sem("oT_tr"), sem("oT_ready"), sem("op_done"), sem("res_ready")
        x1_ss, h2_ready, h2T_tr, h2T_ready = sem("x1_ss"), sem("h2_ready"), sem("h2T_tr"), sem("h2T_ready")
        h2_stored = sem("h2_stored")
        lg_done, lg_read, nv_ready, e4_ready, route_ready = (
            sem("lg_done"), sem("lg_read"), sem("nv_ready"), sem("e4_ready"), sem("route_ready"))
        rank_done, pos_ready, GT_tr, GT_ready, bd_done, acc_ready, acc_stored = (
            sem("rank_done"), sem("pos_ready"), sem("GT_tr"), sem("GT_ready"), sem("bd_done"), sem("acc_ready"),
            sem("acc_stored"))
        cnt_done, nbc_ready, cum_done, table_ready = (
            sem("cnt_done"), sem("nbc_ready"), sem("cum_done"), sem("table_ready"))
        zero_ready = sem("zero_ready")
        idx_step, hot_ready, slot_done, gidx_ready, gathered = (
            sem("idx_step"), sem("hot_ready"), sem("slot_done"), sem("gidx_ready"), sem("gathered"))
        xr_tr, xg_ready, xu_ready = sem("xr_tr"), sem("xg_ready"), sem("xu_ready")
        gate_used, up_used, down_used = sem("gate_used"), sem("up_used"), sem("down_used")
        g_step, g_ready, sig_ready, u_step, mid_ready = (
            sem("g_step"), sem("g_ready"), sem("sig_ready"), sem("u_step"), sem("mid_ready"))
        hi_ready, lo_ready, mid_hi_ready, mid_lo_ready = (
            sem("hi_ready"), sem("lo_ready"), sem("mid_hi_ready"), sem("mid_lo_ready"))
        pool_turn = sem("pool_turn")
        g_read, u_read, now_ready, y_ready, scattered = (
            sem("g_read"), sem("u_read"), sem("now_ready"), sem("y_ready"), sem("scattered"))

        NCONST = 4
        ORDER = (0, 1, 3, 4, 2)
        h2_dram = h2_rows
        block = ctx.enter_context(nc.Block())

        def psum_pair(b, n):
            return [bank[b + i][:, 0:4 * n].rearrange("p (c s) -> p c s", c=4) for i in range(2)]

        gate_ps, up_ps, xt_ps = psum_pair(0, SLOTS), psum_pair(2, SLOTS), psum_pair(6, SLOTS)
        y_ps = [bank[4], bank[5]]
        slot_ps = bank[6][0:SLOTS, 4 * SLOTS:4 * SLOTS + 3]

        @block.sync
        def _(sp):
            for t in range(T):
                sp.dma_start(xres[:, t, :], x[t * P:(t + 1) * P, :]).then_inc(x_in[t], 16)
                if t == 0:
                    sp.dma_start(K[:, :], consts).then_inc(K_in, 16)
                    sp.dma_start(cols[:, :], cols_c).then_inc(cols_in, 16)
                    sp.dma_start(w_in_sb[:, 0, :], w_in[0:P, :]).then_inc(win_in[0], 16)
            for c in range(1, C):
                sp.dma_start(w_in_sb[:, c, :], w_in[c * P:(c + 1) * P, :]).then_inc(win_in[c], 16)
                if c == 2:
                    sp.dma_start(rope, rope_c).then_inc(const_in, 16)
                    sp.dma_start(vecs[:, :], vecs_c.to_broadcast((P, V_W))).then_inc(const_in, 16)
                    sp.dma_start(rb[:, :], router_b).then_inc(const_in, 16)
                    sp.dma_start(R[:, :, :, :].rearrange("p t e k -> p t (e k)"), slot_c).then_inc(const_in, 16)

            def load(dst, src, e, j, arrived):
                s = src[e, 2 * j * P:(2 * j + 2) * P, :] if isinstance(e, int) else \
                    src[bass.ds(e, 1), 2 * j * P:(2 * j + 2) * P, :].rearrange("a r n -> (a r) n")
                sp.dma_start(dst[:, 2 * j:2 * j + 2, :], s.rearrange("(c p) n -> p c n", p=P)).then_inc(arrived[j], 16)

            sp.wait_ge(proj_done, 5 * T)
            sp.dma_start(bd, b_down).then_inc(bd_in, 16)
            sp.wait_ge(qk_rope, T)
            sp.wait_ge(qkT_tr, 4 * T)
            sp.dma_start(w_out_sb, w_out.rearrange("(c p) n -> p c n", p=P)).then_inc(wout_in, 16)
            for j in range(3):
                load(wg, w_gate, 0, j, wg_in)
            sp.wait_ge(pv_done, NU)
            sp.dma_start(bias, bias_c).then_inc(bias_in, 16)
            for j in (2, 3):
                load(wu, w_up, 0, j, wu_in)
            sp.wait_ge(op_done, 2 * T)
            for j in range(C // 2):
                load(wd, w_down, 0, j, wd_in)
            load(wu, w_up, 0, 1, wu_in)
            sp.wait_ge(lg_done, T)
            load(wu, w_up, 0, 0, wu_in)
            sp.wait_ge(bd_done, 2 * T)
            load(wg, w_gate, 0, 3, wg_in)

            def gate_in(b, e):
                for j in range(C // 2):
                    sp.wait_ge(gate_used, (b - 1) * C + 2 * j + 2)
                    load(wg, w_gate, e, j, wg_in)

            def up_in(b, e):
                for j in range(C // 2):
                    sp.wait_ge(up_used, (b - 1) * C + 2 * j + 2)
                    load(wu, w_up, e, j, wu_in)

            def down_in(b, e):
                for j in range(C // 2):
                    sp.wait_ge(lo_ready, (b - 1) * UNITS + RING * j + RING)
                    load(wd, w_down, e, j, wd_in)

            gate_in(1, 1)
            up_in(1, 1)
            sp.wait_ge(table_ready, 1)
            n = sp.value_load(further[0:1, 0:1], min_val=0, max_val=OVER) + E
            with sp.Fori(1, n - 1) as i:
                e_now = sp.value_load(tab_ei[0:1, bass.ds(i, 1)], min_val=0, max_val=E - 1)
                e_next = sp.value_load(tab_ei[0:1, bass.ds(i + 1, 1)], min_val=0, max_val=E - 1)
                gate_in(i + 1, e_next)
                down_in(i, e_now)
                up_in(i + 1, e_next)
            e_last = sp.value_load(tab_ei[0:1, bass.ds(n - 1, 1)], min_val=0, max_val=E - 1)
            down_in(n - 1, e_last)

        @block.tensor
        def _(pe):
            mm, tr = nc.tensor.matmul, nc.tensor.transpose
            pe.wait_ge(K_in, 16)

            for u in range(2 * T):
                t, h = divmod(u, 2)
                pe.wait_ge(x_in[t], 16)
                if u >= 3:
                    pe.wait_ge(xT_ready, u - 2)
                for j in range(4):
                    last = tr(bank[5 + u % 3][:, j * P:(j + 1) * P], xres[:, t, (4 * h + j) * P:(4 * h + j + 1) * P], ident)
                last.then_inc(xT_tr, 1)

            def proj(t, g, c):
                n0, n1 = 512 * g, min(512 * g + 512, WIN)
                last = mm(bank[g][:, 0:n1 - n0], xT[:, c, t * P:(t + 1) * P], w_in_sb[:, c, n0:n1],
                          start=(c == 0), stop=(c == C - 1))
                if c == C - 1:
                    last.then_inc(proj_done, 1)

            def qk_transposes(t):
                pe.wait_ge(qk_rope, t + 1)
                for k in range(4):
                    w = 4 * t + k
                    pe.wait_ge(xT_ready, 2 * T)
                    if w >= 3:
                        pe.wait_ge(qkT_ready, w - 2)
                    for j in range(4 * k, min(4 * k + 4, NCH)):
                        last = tr(bank[5 + w % 3][:, (j % 4) * P:(j % 4 + 1) * P],
                                  qk[t % 2][:, 2 * j:2 * j + 2, :].rearrange("p a d -> p (a d)"), ident)
                    last.then_inc(qkT_tr, 1)

            for c in range(C):
                pe.wait_ge(win_in[c], 16)
                pe.wait_ge(xT_ready, 1 + c // 4)
                for g in ORDER:
                    proj(0, g, c)
            for t in range(1, T):
                pe.wait_ge(xT_ready, 2 * t + 2)
                for k, g in enumerate(ORDER):
                    pe.wait_ge(proj_out, 5 * (t - 1) + k + 1)
                    for c in range(C):
                        proj(t, g, c)
                qk_transposes(t - 1)
            qk_transposes(T - 1)

            def scores(n):
                qt, p = divmod(n, PAIRS)
                if n >= 2:
                    pe.wait_ge(exp_done, 2 * n - 2)
                kc = 4 + p if p < 4 else 12
                qc = p if p < 4 else 8 + p - 4
                for m in range(2):
                    r = slice(HD * m, HD * m + HD)
                    last = mm(bank[2 * (n % 2) + m][:, :], qkT[r, qc, qt * P:(qt + 1) * P], qkT[r, kc, :],
                              start=True, stop=True)
                last.then_inc(sc_done, 1)

            def p_transposes(n):
                qt, p = divmod(n, PAIRS)
                if n >= 1:
                    pe.wait_ge(pT_act, n)
                if p < 4:
                    if qt >= 1:
                        pe.wait_ge(pT_dve, 4 * qt)
                    pe.wait_ge(comb_done, 4 * qt + p + 1)
                else:
                    pe.wait_ge(exp_done, 2 * n + 2)
                    if n % PAIRS >= 5 or qt >= 1:
                        pe.wait_ge(pT_dve, 4 * qt + p - 4)
                for m in range(1 if p < 4 else 2):
                    for j in range(4):
                        last = tr(bank[4 + m][:, j * P:(j + 1) * P], prob[:, n % 3, m, j * P:(j + 1) * P], ident)
                last.then_inc(pT_tr, 1)

            def pv(n):
                qt, p = divmod(n, PAIRS)
                pe.wait_ge(pT_act, n + 1)
                o = bank[6][:, (n % 4) * P:(n % 4 + 1) * P]
                if p < 4:
                    if p >= 1:
                        pe.wait_ge(oA_out, 4 * qt + p)
                    elif qt >= 1:
                        pe.wait_ge(oB_out, 4 * qt)
                    for j in range(4):
                        last = mm(o, probT[:, n % 2, 0, j, :], V[:, j, p * P:(p + 1) * P], start=(j == 0), stop=(j == 3))
                else:
                    pe.wait_ge(pT_dve, 4 * qt + p - 3)
                    if p == 4:
                        pe.wait_ge(oA_out, 4 * qt + 4)
                    else:
                        pe.wait_ge(oB_out, 4 * qt + p - 4)
                    for m in range(2):
                        for j in range(4):
                            last = mm(o[:, m * HD:(m + 1) * HD], probT[:, n % 2, m, j, :],
                                      V[:, j, 512 + m * HD:512 + (m + 1) * HD], start=(j == 0), stop=(j == 3))
                last.then_inc(pv_done, 1)

            def after(t, k):
                b7 = bank[7]
                if k == 0:
                    pe.wait_ge(o_ready, t + 1)
                    if t == 0:
                        pe.wait_ge(qkT_ready, 4 * T)
                    else:
                        pe.wait_ge(acc_ready, 2 * t)
                elif k == 1:
                    pe.wait_ge(oT_ready, 2 * t + 1)
                if k < 2:
                    for j in range(4):
                        last = tr(b7[:, j * P:(j + 1) * P], o_nat[:, t, (4 * k + j) * P:(4 * k + j + 1) * P], ident)
                    last.then_inc(oT_tr, 1)
                elif k < 4:
                    pe.wait_ge(oT_ready, 2 * t + 2)
                    pe.wait_ge(wout_in, 16)
                    if k == 3:
                        pe.wait_ge(res_ready, 2 * t + 1)
                    for c in range(C):
                        last = mm(b7[:, :], oT[:, t % 2, c, :], w_out_sb[:, c, (k - 2) * 512:(k - 1) * 512],
                                  start=(c == 0), stop=(c == C - 1))
                    last.then_inc(op_done, 1)
                elif k < 6:
                    pe.wait_ge(h2_ready, t + 1)
                    if k == 4:
                        pe.wait_ge(res_ready, 2 * t + 2)
                    else:
                        pe.wait_ge(h2T_ready, 2 * t + 1)
                    for j in range(4):
                        last = tr(b7[:, j * P:(j + 1) * P], o_nat[:, t, (4 * (k - 4) + j) * P:(4 * (k - 4) + j + 1) * P], ident)
                    last.then_inc(h2T_tr, 1)
                elif k == 6:
                    pe.wait_ge(h2T_ready, 2 * t + 2)
                    for c in range(C):
                        mm(b7[:, 0:E], h2T[:, c, :], rw[:, c, :], start=(c == 0), stop=False)
                    pe.wait_ge(const_in, 16 * NCONST)
                    mm(b7[:, 0:E], K[0:1, K_ONE:K_ONE + P], rb[:, :], start=False, stop=True).then_inc(lg_done, 1)
                elif k == 7:
                    pe.wait_ge(route_ready, t + 1)
                    for s in range(t):
                        mm(b7[:, 0:E], K[:, K_ONE:K_ONE + P], M[:, s, :], start=(s == 0), stop=False)
                    mm(b7[:, 0:E], K[:, K_TRI:K_TRI + P], M[:, t, :], start=(t == 0), stop=True).then_inc(rank_done, 1)
                    pe.wait_ge(pos_ready, t + 1)
                    tr(b7[0:E, P:2 * P], R[:, t, :, 1], ident).then_inc(GT_tr, 1)
                else:
                    pe.wait_ge(GT_ready, t + 1)
                    pe.wait_ge(bd_in, 16)
                    if k == 9:
                        pe.wait_ge(acc_ready, 2 * t + 1)
                    mm(b7[:, :], GT[:, :], bd[:, (k - 8) * 512:(k - 7) * 512], start=True, stop=True).then_inc(bd_done, 1)

            pe.wait_ge(qkT_ready, 4 * T)
            pe.wait_ge(proj_out, 5 * T)
            scores(0)
            scores(1)
            for n in range(NU):
                if n + 2 < NU:
                    scores(n + 2)
                qt, p = divmod(n, PAIRS)
                p_transposes(n)
                if n >= 1:
                    pv(n - 1)
                if qt >= 1:
                    if p >= 1:
                        after(qt - 1, p - 1)
                    if p == PAIRS - 1:
                        for k in (7, 8, 9):
                            after(qt - 1, k)
            pv(NU - 1)
            for k in range(8):
                after(T - 1, k)

            for t in range(T):
                last = mm(bank[0][0:E, 0:1], M[:, t, :], K[:, K_ONE:K_ONE + 1], start=(t == 0), stop=(t == T - 1))
            last.then_inc(cnt_done, 1)

            def slot_sums(b):
                pe.wait_ge(hot_ready, b + 1)
                if not isinstance(b, int) or b > 0:
                    pe.wait_ge(gidx_ready, b)
                for t in range(T):
                    last = mm(slot_ps, onehot[:, t, :], Rcur[:, t, :], start=(t == 0), stop=(t == T - 1))
                last.then_inc(slot_done, 1)

            def row_transposes(b):
                pe.wait_ge(gathered, 16 * (b + 1))
                if not isinstance(b, int) or b > 0:
                    pe.wait_ge(xg_ready, b)
                for c in range(C):
                    last = tr(xt_ps[c // 4][:, c % 4, :], xrow[0:SLOTS, c * P:(c + 1) * P], ident[0:SLOTS, 0:SLOTS])
                last.then_inc(xr_tr, 1)

            def product(w, arrived, xt, ps, used, b):
                for c in range(C):
                    if c % 2 == 0:
                        pe.wait_ge(arrived[c // 2], 16 * (b + 1))
                    for f in range(C):
                        last = mm(ps[f // 4][:, f % 4, :], w[:, c, f * P:(f + 1) * P], xt[:, c, :],
                                  start=(c == 0 and f % 4 == 0), stop=(c == C - 1), skip_group_check=True)
                    last.then_inc(used, 1)

            def gate(b):
                pe.wait_ge(xg_ready, b + 1)
                if not isinstance(b, int) or b > 0:
                    pe.wait_ge(g_read, b)
                product(wg, wg_in, xg, gate_ps, gate_used, b)

            def up(b):
                pe.wait_ge(xu_ready, b + 1)
                if not isinstance(b, int) or b > 0:
                    pe.wait_ge(u_read, b)
                product(wu, wu_in, xu, up_ps, up_used, b)

            def down(b):
                pe.wait_ge(mid_lo_ready, b + 1)
                if not isinstance(b, int) or b > 0:
                    pe.wait_ge(y_ready, b)
                for u in range(UNITS):
                    c, h = divmod(u, 2)
                    y = y_ps[h][0:SLOTS, :]
                    pe.wait_ge(lo_ready, UNITS * b + u + 1)
                    mm(y, mid_hi[:, c, :], w_hi[:, u % RING, :], start=(c == 0), stop=False)
                    mm(y, mid_hi[:, c, :], w_lo[:, u % RING, :], start=False, stop=False)
                    mm(y, mid_lo[:, c, :], w_hi[:, u % RING, :], start=False, stop=(c == C - 1)).then_inc(down_used, 1)

            slot_sums(0)
            pe.wait_ge(nbc_ready, 1)
            mm(bank[0][:, 0:2 * E], nbc[:, :], K[0:E, K_CUM:K_CUM + 2 * E], start=True, stop=True).then_inc(cum_done, 1)
            for k in (8, 9):
                after(T - 1, k)
            pe.wait_ge(acc_ready, 2 * T)
            row_transposes(0)
            slot_sums(1)
            pe.wait_ge(table_ready, 1)
            gate(0)
            row_transposes(1)
            slot_sums(2)
            up(0)
            n_blocks = pe.value_load(further[0:1, 0:1], min_val=0, max_val=OVER) + E
            with pe.Fori(0, n_blocks - 1) as i:
                gate(i + 1)
                row_transposes(i + 2)
                slot_sums(i + 3)
                down(i)
                up(i + 1)
            down(n_blocks - 1)

        @block.scalar
        def _(act):
            A = nc.scalar.activation
            steps = [0]

            def link(ins):
                steps[0] += 1
                ins.then_inc(act_step, 1)
                act.wait_ge(act_step, steps[0])

            for t in range(T):
                act.wait_ge(x_in[t], 16)
                if t:
                    act.wait_ge(xss, t)
                A(xsq, xres[:, t, :], ACT.Square, accum_out=st[:, t:t + 1]).then_inc(xss, 1)
            act.wait_ge(lam_dot, 1)
            A(st[:, 10:12], st[:, 8:10], ACT.Exp).then_inc(lam_exp, 1)

            def proj_evacuate(t):
                act.wait_ge(root_ready, 1)
                if t >= 2:
                    act.wait_ge(qkT_tr, 4 * (t - 1))
                for k, g in enumerate(ORDER):
                    r1 = st[:, 4 + t:5 + t]
                    b = t % 2
                    if k == 4:
                        if t:
                            act.wait_ge(qk_rope, t)
                        act.wait_ge(proj_out, 5 * t + 4)
                        A(t1, qk[b], ACT.Square).then_inc(qk_sq, 1)
                    act.wait_ge(proj_done, 5 * t + k + 1)
                    if g < 2:
                        A(qk[b][:, 8 * g:8 * g + 8, :].rearrange("p n d -> p (n d)"), bank[g][:, :], ACT.Copy,
                          scale=r1).then_inc(proj_out, 1)
                    elif g == 2:
                        A(V[:, t, 0:512], bank[g][:, :], ACT.Copy, scale=r1).then_inc(proj_out, 1)
                    elif g == 3:
                        A(qk[b][:, 16:24, :].rearrange("p (j g) d -> p g j d", g=2),
                          bank[g][:, :].rearrange("p (g j d) -> p g j d", g=2, j=4), ACT.Copy,
                          scale=r1).then_inc(proj_out, 1)
                    else:
                        link(A(qk[b][:, 24:26, :].rearrange("p n d -> p (n d)"), bank[g][:, 0:128], ACT.Copy, scale=r1))
                        A(V[:, t, 512:640], bank[g][:, 128:256], ACT.Copy, scale=r1).then_inc(proj_out, 1)
            def qkT_evacuate(t):
                for k in range(4):
                    act.wait_ge(qkT_tr, 4 * t + k + 1)
                    n = min(4, NCH - 4 * k)
                    A(qkT[:, 4 * k:4 * k + n, t * P:(t + 1) * P],
                      bank[5 + (4 * t + k) % 3][:, 0:n * P].rearrange("p (j s) -> p j s", j=n), ACT.Copy).then_inc(qkT_ready, 1)

            for t in range(T):
                proj_evacuate(t)
                if t:
                    qkT_evacuate(t - 1)
            qkT_evacuate(T - 1)

            def exps(n):
                act.wait_ge(max_ready, n + 1)
                if n >= 3:
                    act.wait_ge(pT_tr, n - 2)
                if n >= 4:
                    act.wait_ge(rcp_done, n - 3)
                for m in range(2):
                    A(prob[:, n % 3, m, :], bank[2 * (n % 2) + m][:, :], ACT.Exp, bias=nmx[:, n % 4, m:m + 1],
                      scale=SCALE, accum_out=rs[:, n % 4, m:m + 1]).then_inc(exp_done, 1)

            def pT_evacuate(n):
                act.wait_ge(pT_tr, n + 1)
                if n >= 2:
                    act.wait_ge(pv_done, n - 1)
                A(probT[:, n % 2, 0, :, :].rearrange("p j q -> p (j q)"), bank[4][:, :], ACT.Copy).then_inc(pT_act, 1)

            def oA_evacuate(n):
                qt, p = divmod(n, PAIRS)
                if p < 4:
                    act.wait_ge(pv_done, n + 1)
                    A(o_nat[:, qt, p * P:(p + 1) * P], bank[6][:, (n % 4) * P:(n % 4 + 1) * P], ACT.Copy).then_inc(oA_out, 1)

            def after(t, k):
                if k < 2:
                    act.wait_ge(oT_tr, 2 * t + k + 1)
                    if t >= 2:
                        act.wait_ge(op_done, 2 * (t - 1))
                    A(oT[:, t % 2, 4 * k:4 * k + 4, :].rearrange("p c s -> p (c s)"), bank[7][:, :], ACT.Copy).then_inc(oT_ready, 1)
                elif k == 3:
                    act.wait_ge(res_ready, 2 * t + 2)
                    if t:
                        act.wait_ge(lg_done, t)
                    A(h2T.rearrange("p c s -> p (c s)"), xres[:, t, :], ACT.Square, accum_out=st[:, 16 + t:17 + t]).then_inc(x1_ss, 1)
                elif k == 6:
                    act.wait_ge(nv_ready, t + 1)
                    A(e4[:, 0:4], v8[:, 0:4], ACT.Exp, bias=e4[:, 4:5], accum_out=e4[:, 5:6]).then_inc(e4_ready, 1)
                elif k == 7:
                    act.wait_ge(GT_tr, t + 1)
                    if t:
                        act.wait_ge(bd_done, 2 * t)
                    A(GT[:, :], bank[7][0:E, P:2 * P], ACT.Copy).then_inc(GT_ready, 1)

            exps(0)
            exps(1)
            for n in range(NU):
                if n + 2 < NU:
                    exps(n + 2)
                qt, p = divmod(n, PAIRS)
                pT_evacuate(n)
                if n >= 1:
                    oA_evacuate(n - 1)
                if qt >= 1:
                    if p >= 1:
                        after(qt - 1, p - 1)
                    if p == PAIRS - 1:
                        after(qt - 1, 7)
            for k in range(8):
                after(T - 1, k)

            def copy_xT(b):
                act.wait_ge(xg_ready, b + 1)
                if not isinstance(b, int) or b > 0:
                    act.wait_ge(up_used, C * b)
                A(xu, xg, ACT.Copy).then_inc(xu_ready, 1)

            def sigmoid(b):
                act.wait_ge(g_ready, b + 1)
                A(sig, gact, ACT.Sigmoid, scale=ALPHA).then_inc(sig_ready, 1)

            def high_parts(b, u0, u1):
                for u in range(u0, u1):
                    c, h = divmod(u, 2)
                    if u % RING == 0:
                        act.wait_ge(wd_in[u // RING], 16 * (b + 1))
                    if not isinstance(b, int) or b > 0 or u >= RING:
                        act.wait_ge(down_used, UNITS * b + u + 1 - RING)
                    A(w_hi[:, u % RING, :], wd[:, c, h * HALF:(h + 1) * HALF], ACT.Copy).then_inc(hi_ready, 1)

            def mid_high(b):
                act.wait_ge(mid_ready, b + 1)
                if not isinstance(b, int) or b > 0:
                    act.wait_ge(down_used, UNITS * b)
                A(mid_hi[:, :, :], mid, ACT.Copy).then_inc(mid_hi_ready, 1)

            def rows_out(b):
                act.wait_ge(down_used, UNITS * (b + 1))
                act.wait_ge(now_ready, b + 1)
                if isinstance(b, int) and b == 0:
                    act.wait_ge(acc_stored, 16 * (T + 1))
                else:
                    act.wait_ge(scattered, 16 * b)
                A(y_sb[0:SLOTS, 0:512], y_ps[0][0:SLOTS, :], ACT.Copy, scale=gnow[:, 0:1])
                A(y_sb[0:SLOTS, 512:D], y_ps[1][0:SLOTS, :], ACT.Copy, scale=gnow[:, 0:1]).then_inc(y_ready, 1)

            copy_xT(0)
            sigmoid(0)
            copy_xT(1)
            mid_high(0)
            high_parts(0, 0, RING)
            act.wait_ge(table_ready, 1)
            n_blocks = act.value_load(further[0:1, 0:1], min_val=0, max_val=OVER) + E
            with act.Fori(0, n_blocks - 1) as i:
                high_parts(i, RING, UNITS)
                rows_out(i)
                sigmoid(i + 1)
                copy_xT(i + 2)
                mid_high(i + 1)
                high_parts(i + 1, 0, RING)
            high_parts(n_blocks - 1, RING, UNITS)
            rows_out(n_blocks - 1)

        @block.vector
        def _(dve):
            v = nc.vector
            steps = [0]

            def link(ins):
                steps[0] += 1
                ins.then_inc(dve_step, 1)
                dve.wait_ge(dve_step, steps[0])

            asked = [0]

            def rms(out, ss, width):
                asked[0] += 1
                v.tensor_scalar(out, ss, 1.0 / width, EPS, ALU.mult, ALU.add).then_inc(mean_ready, 1)
                dve.wait_ge(root_ready, asked[0])

            dve.wait_ge(cols_in, 16)
            dve.wait_ge(K_in, 16)
            g1 = cols[:, C_G1:C_G1 + C]
            g2 = cols[:, C_G2:C_G2 + C]
            for u in range(2 * T):
                t, h = divmod(u, 2)
                dve.wait_ge(xT_tr, u + 1)
                v.tensor_tensor(xT[:, 4 * h:4 * h + 4, t * P:(t + 1) * P],
                                bank[5 + u % 3][:, :].rearrange("p (c s) -> p c s", c=4),
                                g1[:, 4 * h:4 * h + 4].unsqueeze(2).to_broadcast((P, 4, P)), ALU.mult).then_inc(xT_ready, 1)
            dve.wait_ge(xss, T)
            rms(st[:, 4:8], st[:, 0:4], D)
            dve.wait_ge(const_in, 16 * NCONST)
            link(v.tensor_tensor(sq[:, 0:HD], lamv[:, 0, :], lamv[:, 1, :], ALU.mult))
            link(v.tensor_tensor(sq[:, HD:2 * HD], lamv[:, 2, :], lamv[:, 3, :], ALU.mult))
            v.tensor_reduce(st[:, 8:10], sq[:, 0:2 * HD].rearrange("p (a d) -> p a d", a=2), AX.X, ALU.add).then_inc(lam_dot, 1)
            dve.wait_ge(lam_exp, 1)
            link(v.tensor_tensor(st[:, 12:13], st[:, 11:12], st[:, 10:11], ALU.subtract))
            link(v.tensor_scalar(st[:, 12:13], st[:, 12:13], -LAM_INIT, None, ALU.add))
            link(v.tensor_scalar(subg[:, :], vecs[:, V_SUB:V_SUB + 128], 1.0 - LAM_INIT, None, ALU.mult))

            kinds = ((0, 8, 0), (8, 16, 0), (16, 24, 1), (24, 26, 1))

            def rotate(t):
                b = t % 2
                n = qk[b]
                for k, (_, _, tab) in enumerate(kinds):
                    for s in range(2):
                        lastk = v.tensor_tensor(ropeg[:, 2 * k + s, :], rope[:, t, (2 * tab + s) * HD:(2 * tab + s + 1) * HD],
                                                gain[:, k, :], ALU.mult)
                link(lastk)
                dve.wait_ge(qk_sq, t + 1)
                link(v.tensor_reduce(ssq[:, :], t1, AX.X, ALU.add))
                rms(rsq[:, :], ssq[:, :], HD)
                link(v.tensor_tensor(n, n, rsq[:, :].unsqueeze(2).to_broadcast((P, NQK, HD)), ALU.mult))
                for k, (lo, hi, _) in enumerate(kinds):
                    for s, dst in ((0, t1), (1, t2)):
                        lastk = v.tensor_tensor(dst[:, lo:hi, :], n[:, lo:hi, :],
                                                ropeg[:, 2 * k + s, :].unsqueeze(1).to_broadcast((P, hi - lo, HD)), ALU.mult)
                link(lastk)
                h = HD // 2
                v.tensor_tensor(n[:, :, 0:h], t1[:, :, 0:h], t2[:, :, h:HD], ALU.add)
                v.tensor_tensor(n[:, :, h:HD], t1[:, :, h:HD], t2[:, :, 0:h], ALU.add).then_inc(qk_rope, 1)

            for t in range(T):
                rotate(t)

            def row_max(n):
                dve.wait_ge(sc_done, n + 1)
                for m in range(2):
                    lastk = v.tensor_reduce(mx[:, n % 4, m:m + 1], bank[2 * (n % 2) + m][:, :], AX.X, ALU.max)
                link(lastk)
                v.tensor_scalar(nmx[:, n % 4, :], mx[:, n % 4, :], -SCALE, None, ALU.mult).then_inc(max_ready, 1)

            def combine(n):
                qt, p = divmod(n, PAIRS)
                dve.wait_ge(exp_done, 2 * n + 2)
                if p >= 4:
                    v.reciprocal(rr[:, n % 4, :], rs[:, n % 4, :]).then_inc(rcp_done, 1)
                    return
                v.reciprocal(rr[:, n % 4, :], rs[:, n % 4, :]).then_inc(rcp_done, 1)
                dve.wait_ge(rcp_done, n + 1)
                v.tensor_tensor(nla[:, n % 4:n % 4 + 1], rr[:, n % 4, 1:2], st[:, 12:13], ALU.mult)
                a, c = prob[:, n % 3, 0, :], prob[:, n % 3, 1, :]
                link(v.tensor_scalar(a, a, rr[:, n % 4, 0:1], None, ALU.mult))
                v.scalar_tensor_tensor(out=a, in0=c, scalar=nla[:, n % 4:n % 4 + 1], in1=a, op0=ALU.mult,
                                       op1=ALU.add).then_inc(comb_done, 1)

            def pT_evacuate(n):
                if n % PAIRS >= 4:
                    dve.wait_ge(pT_tr, n + 1)
                    if n >= 2:
                        dve.wait_ge(pv_done, n - 1)
                    v.tensor_copy(probT[:, n % 2, 1, :, :].rearrange("p j q -> p (j q)"), bank[5][:, :]).then_inc(pT_dve, 1)

            def oB_evacuate(n):
                qt, p = divmod(n, PAIRS)
                if p >= 4:
                    dve.wait_ge(pv_done, n + 1)
                    dve.wait_ge(rcp_done, n + 1)
                    v.tensor_tensor(o_nat[:, qt, 512:1024].rearrange("p (g j d) -> p g j d", g=2, j=4)[:, :, p - 4, :],
                                    bank[6][:, (n % 4) * P:(n % 4 + 1) * P].rearrange("p (m d) -> p m d", m=2),
                                    rr[:, n % 4, :].unsqueeze(2).to_broadcast((P, 2, HD)), ALU.mult).then_inc(oB_out, 1)

            def sub_norm(qt):
                dve.wait_ge(oA_out, 4 * qt + 4)
                o = o_nat[:, qt, 0:512].rearrange("p (h d) -> p h d", h=4)
                s3 = sq.rearrange("p (h d) -> p h d", h=4)
                link(v.tensor_tensor(s3, o, o, ALU.mult))
                link(v.tensor_reduce(sub[:, 0:4], s3, AX.X, ALU.add))
                rms(sub[:, 4:8], sub[:, 0:4], 128)
                link(v.tensor_tensor(o, o, sub[:, 4:8].unsqueeze(2).to_broadcast((P, 4, P)), ALU.mult))
                link(v.tensor_tensor(o, o, subg[:, :].unsqueeze(1).to_broadcast((P, 4, P)), ALU.mult))

            def after(t, k):
                b7 = bank[7]
                if k in (2, 3):
                    h = k - 2
                    dve.wait_ge(op_done, 2 * t + h + 1)
                    xx = xres[:, t, h * 512:(h + 1) * 512]
                    v.tensor_tensor(xx, b7[:, :], xx, ALU.add).then_inc(res_ready, 1)
                    if k == 3:
                        dve.wait_ge(x1_ss, t + 1)
                        rms(st[:, 20 + t:21 + t], st[:, 16 + t:17 + t], D)
                        dve.wait_ge(oT_tr, 2 * t + 2)
                        v.tensor_scalar(o_nat[:, t, :], xres[:, t, :], st[:, 20 + t:21 + t], None, ALU.mult).then_inc(h2_ready, 1)
                elif k in (4, 5):
                    h = k - 4
                    dve.wait_ge(h2T_tr, 2 * t + h + 1)
                    if t:
                        dve.wait_ge(lg_done, t)
                    v.tensor_tensor(h2T[:, 4 * h:4 * h + 4, :], b7[:, :].rearrange("p (c s) -> p c s", c=4),
                                    g2[:, 4 * h:4 * h + 4].unsqueeze(2).to_broadcast((P, 4, P)), ALU.mult).then_inc(h2T_ready, 1)
                elif k == 6:
                    dve.wait_ge(lg_done, t + 1)
                    link(v.tensor_copy(lg[:, :], b7[:, 0:E]))
                    link(v.max(v8[:, :], lg[:, :]))
                    v.tensor_scalar(e4[:, 4:5], v8[:, 0:1], -1.0, None, ALU.mult).then_inc(nv_ready, 1)
                    link(v.max_index(i8[:, :], v8[:, :], lg[:, :]))
                    link(v.tensor_copy(i8f[:, :], i8[:, :]))
                    link(v.tensor_tensor(oh4[:, :, :], K[:, K_E32:K_E32 + E].unsqueeze(1).to_broadcast((P, 4, E)),
                                         i8f[:, 0:4].unsqueeze(2).to_broadcast((P, 4, E)), ALU.is_equal))
                    v.tensor_reduce(M[:, t, :], oh4[:, :, :].rearrange("p j e -> p e j"), AX.X, ALU.add)
                    dve.wait_ge(e4_ready, t + 1)
                    link(v.reciprocal(e4[:, 6:7], e4[:, 5:6]))
                    link(v.tensor_scalar(g4[:, :], e4[:, 0:4], e4[:, 6:7], None, ALU.mult))
                    link(v.tensor_tensor(ohg[:, :, :], oh4[:, :, :], g4[:, :].unsqueeze(2).to_broadcast((P, 4, E)), ALU.mult))
                    v.tensor_reduce(R[:, t, :, 1], ohg[:, :, :].rearrange("p j e -> p e j"), AX.X, ALU.add).then_inc(route_ready, 1)
                elif k == 7:
                    dve.wait_ge(rank_done, t + 1)
                    v.scalar_tensor_tensor(out=pos[:, t, :], in0=M[:, t, :], scalar=-FAR, in1=b7[:, 0:E], op0=ALU.mult,
                                           op1=ALU.add).then_inc(pos_ready, 1)
                elif k in (8, 9):
                    h = k - 8
                    dve.wait_ge(bd_done, 2 * t + h + 1)
                    if h == 0:
                        dve.wait_ge(h2_ready, t + 1)
                    xx = xres[:, t, h * 512:(h + 1) * 512]
                    v.tensor_tensor(xx, b7[:, :], xx, ALU.add).then_inc(acc_ready, 1)

            row_max(0)
            row_max(1)
            combine(0)
            for n in range(NU):
                qt, p = divmod(n, PAIRS)
                if n + 2 < NU:
                    row_max(n + 2)
                if n + 1 < NU:
                    combine(n + 1)
                pT_evacuate(n)
                if n >= 1:
                    oB_evacuate(n - 1)
                    if (n - 1) % PAIRS == 4:
                        sub_norm(qt)
                    if (n - 1) % PAIRS == PAIRS - 1:
                        v.tensor_copy(sub[:, 0:1], sub[:, 4:5]).then_inc(o_ready, 1)
                        dve.wait_ge(oB_out, 4 * qt)
                if qt >= 1:
                    if p >= 1:
                        after(qt - 1, p - 1)
                    if p == PAIRS - 1:
                        for k in (7, 8, 9):
                            after(qt - 1, k)
            oB_evacuate(NU - 1)
            dve.wait_ge(oB_out, 4 * T)
            v.tensor_copy(sub[:, 0:1], sub[:, 4:5]).then_inc(o_ready, 1)
            for k in range(8):
                after(T - 1, k)

            def mark_slots(b, e):
                if not isinstance(b, int) or b > 0:
                    dve.wait_ge(slot_done, b)
                bc = slice(b, b + 1) if isinstance(b, int) else bass.ds(b, 1)
                ec = slice(e, e + 1) if isinstance(e, int) else bass.ds(e, 1)
                v.tensor_scalar(slot_b[:, :], K[:, K_SLOT:K_SLOT + SLOTS], tab_base[:, bc], None, ALU.add).then_inc(idx_step, 1)
                v.tensor_copy(Rcur[:, :, :], R[:, :, ec, :].rearrange("p t a k -> p t (a k)"))
                dve.wait_ge(idx_step, 3 * b + 1)
                v.tensor_tensor(onehot[:, :, :], slot_b[:, :].unsqueeze(1).to_broadcast((P, T, SLOTS)),
                                pos[:, :, ec].to_broadcast((P, T, SLOTS)), ALU.is_equal).then_inc(hot_ready, 1)

            def slot_info(b):
                bc = slice(b, b + 1) if isinstance(b, int) else bass.ds(b, 1)
                dve.wait_ge(slot_done, b + 1)
                if not isinstance(b, int) or b > 0:
                    dve.wait_ge(gathered, 16 * b)
                v.tensor_copy(si[:, 0:3], slot_ps).then_inc(idx_step, 1)
                dve.wait_ge(idx_step, 3 * b + 2)
                v.tensor_copy(gtab[:, bc], si[:, 1:2])
                v.scalar_tensor_tensor(out=si[:, 3:4], in0=si[:, 2:3], scalar=K[0:SLOTS, K_SPARE:K_SPARE + 1], in1=si[:, 0:1],
                                       op0=ALU.mult, op1=ALU.subtract).then_inc(idx_step, 1)
                dve.wait_ge(idx_step, 3 * b + 3)
                v.scalar_tensor_tensor(out=stab[:, bc], in0=si[:, 3:4], scalar=-1.0, in1=K[0:SLOTS, K_SPARE:K_SPARE + 1],
                                       op0=ALU.mult, op1=ALU.add)
                v.tensor_copy(gidx[:, :], si[:, 0:1]).then_inc(gidx_ready, 1)

            def gained(b):
                dve.wait_ge(xr_tr, b + 1)
                dve.wait_ge(slot_done, b + 2)
                if not isinstance(b, int) or b > 0:
                    dve.wait_ge(gate_used, C * b)
                    dve.wait_ge(xu_ready, b)
                v.tensor_tensor(xg[:, 0:4, :], xt_ps[0], g2[:, 0:4].unsqueeze(2).to_broadcast((P, 4, SLOTS)), ALU.mult)
                v.tensor_tensor(xg[:, 4:8, :], xt_ps[1], g2[:, 4:8].unsqueeze(2).to_broadcast((P, 4, SLOTS)),
                                ALU.mult).then_inc(xg_ready, 1)

            def gates(b, e):
                ec = slice(e, e + 1) if isinstance(e, int) else bass.ds(e, 1)
                if isinstance(b, int) and b == 0:
                    dve.wait_ge(bias_in, 16)
                    dve.wait_ge(h2_stored, 16 * T)
                v.tensor_copy(bgc[:, :].unsqueeze(2), bgate[:, :, ec]).then_inc(g_step, 1)
                v.tensor_copy(buc[:, :].unsqueeze(2), bup[:, :, ec]).then_inc(g_step, 1)
                dve.wait_ge(g_step, 2 * b + 2)
                dve.wait_ge(gate_used, C * (b + 1))
                if not isinstance(b, int) or b > 0:
                    dve.wait_ge(mid_ready, b)
                for i in range(2):
                    last = v.tensor_tensor(gact[:, 4 * i:4 * i + 4, :], gate_ps[i],
                                           bgc[:, 4 * i:4 * i + 4].unsqueeze(2).to_broadcast((P, 4, SLOTS)), ALU.add)
                last.then_inc(g_read, 1)
                dve.wait_ge(g_read, b + 1)
                v.tensor_scalar(gact, gact, LIMIT, None, ALU.min).then_inc(g_ready, 1)

            def middle(b):
                dve.wait_ge(up_used, C * (b + 1))
                for i in range(2):
                    last = v.tensor_tensor(uact[:, 4 * i:4 * i + 4, :], up_ps[i],
                                           buc[:, 4 * i:4 * i + 4].unsqueeze(2).to_broadcast((P, 4, SLOTS)), ALU.add)
                last.then_inc(u_read, 1)
                dve.wait_ge(u_read, b + 1)
                v.tensor_scalar(uact, uact, LIMIT, -LIMIT, ALU.min, ALU.max).then_inc(u_step, 1)
                dve.wait_ge(u_step, 2 * b + 1)
                dve.wait_ge(g_ready, b + 1)
                v.scalar_tensor_tensor(out=uact, in0=uact, scalar=1.0, in1=gact, op0=ALU.add, op1=ALU.mult).then_inc(u_step, 1)
                dve.wait_ge(u_step, 2 * b + 2)
                dve.wait_ge(sig_ready, b + 1)
                if not isinstance(b, int) or b > 0:
                    dve.wait_ge(mid_hi_ready, b)
                v.tensor_tensor(mid, uact, sig, ALU.mult).then_inc(mid_ready, 1)

            def mid_low(b):
                dve.wait_ge(mid_hi_ready, b + 1)
                v.tensor_tensor(mid_lo[:, :, :], mid, mid_hi[:, :, :].bitcast(F32), ALU.subtract).then_inc(mid_lo_ready, 1)

            def low_parts(b, u0, u1):
                for u in range(u0, u1):
                    c, h = divmod(u, 2)
                    dve.wait_ge(hi_ready, UNITS * b + u + 1)
                    v.tensor_tensor(w_lo[:, u % RING, :], wd[:, c, h * HALF:(h + 1) * HALF],
                                    w_hi[:, u % RING, :].bitcast(F32), ALU.subtract).then_inc(lo_ready, 1)

            def now(b):
                bc = slice(b, b + 1) if isinstance(b, int) else bass.ds(b, 1)
                if not isinstance(b, int) or b > 0:
                    dve.wait_ge(scattered, 16 * b)
                v.tensor_copy(gnow[:, :], gtab[:, bc])
                v.tensor_copy(sidx[:, :], stab[:, bc]).then_inc(now_ready, 1)

            link(v.memset(tab_base[:, 0:E], 0.0))
            link(v.tensor_copy(tab_e[:, 0:E], K[:, K_E32:K_E32 + E]))
            v.memset(y_sb[0:SLOTS, :], 0.0).then_inc(zero_ready, 1)
            dve.wait_ge(pos_ready, T)
            mark_slots(0, 0)
            slot_info(0)
            mark_slots(1, 1)
            dve.wait_ge(cnt_done, 1)
            link(v.tensor_copy(cnt[:, 0:1], bank[0][0:E, 0:1]))
            link(v.tensor_tensor(cnt[:, 1:1 + NTHR], K[0:E, K_THR:K_THR + NTHR], cnt[:, 0:1].to_broadcast((E, NTHR)), ALU.is_lt))
            link(v.tensor_reduce(cnt[:, 8:9], cnt[:, 1:1 + NTHR], AX.X, ALU.add))
            v.tensor_scalar(nbc[:, :], K[0:E, K_ONE:K_ONE + P], cnt[:, 8:9], None, ALU.mult).then_inc(nbc_ready, 1)
            for k in (8, 9):
                after(T - 1, k)
            gained(0)
            slot_info(1)
            mark_slots(2, 2)
            dve.wait_ge(cum_done, 1)
            link(v.tensor_copy(cum[:, :], bank[0][:, 0:2 * E]))
            link(v.tensor_tensor(le[:, :, :], cum[:, 0:E].unsqueeze(1).to_broadcast((P, NX, E)),
                                 K[:, K_BIDX:K_BIDX + NX].unsqueeze(2).to_broadcast((P, NX, E)), ALU.is_le))
            v.tensor_copy(btab[:, 3, :], le[:, :, E - 1])
            link(v.tensor_reduce(btab[:, 0, :], le[:, :, :], AX.X, ALU.add))
            link(v.tensor_scalar(tab_e[:, E:NB], btab[:, 0, :], float(E - 1), None, ALU.min))
            link(v.tensor_copy(tab_ei[:, :], tab_e[:, :]))
            link(v.tensor_tensor(le[:, :, :], le[:, :, :], cum[:, E:2 * E].unsqueeze(1).to_broadcast((P, NX, E)), ALU.mult))
            link(v.tensor_reduce(btab[:, 1, :], le[:, :, :], AX.X, ALU.add))
            link(v.tensor_tensor(btab[:, 2, :], K[:, K_BIDX:K_BIDX + NX], btab[:, 1, :], ALU.subtract))
            link(v.tensor_scalar(btab[:, 2, :], btab[:, 2, :], 1.0, float(SLOTS), ALU.add, ALU.mult))
            link(v.scalar_tensor_tensor(out=tab_base[:, E:NB], in0=btab[:, 3, :], scalar=2 * FAR, in1=btab[:, 2, :],
                                        op0=ALU.mult, op1=ALU.add))
            v.tensor_copy(further[:, :], cum[:, E - 1:E]).then_inc(table_ready, 1)
            dve.wait_ge(table_ready, 1)
            gates(0, 0)
            gained(1)
            slot_info(2)
            middle(0)
            now(0)
            mid_low(0)
            low_parts(0, 0, RING)
            n_blocks = dve.value_load(further[0:1, 0:1], min_val=0, max_val=OVER) + E
            with dve.Fori(0, n_blocks - 1) as i:
                e_next = dve.value_load(tab_ei[0:1, bass.ds(i + 1, 1)], min_val=0, max_val=E - 1)
                e_look = dve.value_load(tab_ei[0:1, bass.ds(i + 3, 1)], min_val=0, max_val=E - 1)
                mark_slots(i + 3, e_look)
                low_parts(i, RING, UNITS)
                gates(i + 1, e_next)
                gained(i + 2)
                slot_info(i + 3)
                middle(i + 1)
                now(i + 1)
                mid_low(i + 1)
                low_parts(i + 1, 0, RING)
            low_parts(n_blocks - 1, RING, UNITS)

        @block.gpsimd
        def _(pool):
            asked = [0]

            def root(a, n):
                asked[0] += 1
                pool.wait_ge(mean_ready, asked[0])
                half = K[:, K_HALF:K_HALF + 1]
                nc.gpsimd.tensor_tensor(a, a, half if n == 1 else half.to_broadcast((P, n)), ALU.pow).then_inc(root_ready, 1)

            pool.wait_ge(K_in, 16)
            root(st[:, 4:8], T)
            for t in range(T):
                root(rsq[:, :], NQK)
            root(sub[:, 4:8], 4)
            for t in range(T):
                root(st[:, 20 + t:21 + t], 1)
                if t + 1 < T:
                    root(sub[:, 4:8], 4)
                pool.wait_ge(h2_ready, t + 1)
                pool.dma_start(h2_dram[t * P:(t + 1) * P, :], o_nat[:, t, :]).then_inc(h2_stored, 16)
                if t:
                    pool.wait_ge(acc_ready, 2 * t)
                    pool.dma_start(out[(t - 1) * P:t * P, :], xres[:, t - 1, :]).then_inc(acc_stored, 16)
            pool.wait_ge(zero_ready, 1)
            pool.dma_start(out[SEQ:ROWS, :], y_sb[0:SLOTS, :]).then_inc(acc_stored, 16)
            def gather(b):
                pool.wait_ge(gidx_ready, b + 1)
                if not isinstance(b, int) or b > 0:
                    pool.wait_ge(xr_tr, b)
                pool.sem_inc(pool_turn, 1)
                pool.wait_ge(h2_stored, 16 * T)
                nc.gpsimd.indirect_dma_start(
                    out=xrow[0:SLOTS, :], out_offset=None, in_=h2_dram,
                    in_offset=bass.IndirectOffsetOnAxis(ap=gidx[:, 0:1], axis=0)).then_inc(gathered, 16)

            def scatter(b):
                pool.wait_ge(y_ready, b + 1)
                if not isinstance(b, int) or b > 0:
                    pool.wait_ge(scattered, 16 * b)
                pool.sem_inc(pool_turn, 1)
                pool.wait_ge(acc_stored, 16 * (T + 1))
                nc.gpsimd.indirect_dma_start(
                    out=out, out_offset=bass.IndirectOffsetOnAxis(ap=sidx[:, 0:1], axis=0), in_=y_sb[0:SLOTS, :],
                    in_offset=None, compute_op=ALU.add).then_inc(scattered, 16)

            gather(0)
            pool.wait_ge(acc_ready, 2 * T)
            pool.dma_start(out[(T - 1) * P:T * P, :], xres[:, T - 1, :]).then_inc(acc_stored, 16)
            gather(1)
            gather(2)
            pool.wait_ge(table_ready, 1)
            n_blocks = pool.value_load(further[0:1, 0:1], min_val=0, max_val=OVER) + E
            with pool.Fori(0, n_blocks - 1) as i:
                gather(i + 3)
                scatter(i)
            scatter(n_blocks - 1)
            pool.wait_ge(scattered, 16 * n_blocks)
            pool.wait_ge(gathered, 16 * (n_blocks + 2))


def kernel(x, norm1_g, w_in, a_qnorm_g, a_knorm_g, a_lq1, a_lk1, a_lq2, a_lk2, a_subln_g, b_qnorm_g, b_knorm_g,
           w_out, norm2_g, router_w, router_b, w_gate, b_gate, w_up, b_up, w_down, b_down):
    import concourse.bacc as _bacc
    from concourse.bass_utils import run_bass_kernel_spmd as _run

    nc = _bacc.Bacc("TRN2", target_bir_lowering=False, num_devices=1)

    def per_partition(a):
        a = np.asarray(a)[0]
        return np.moveaxis(a.reshape(-1, C, P), 2, 0).transpose(0, 2, 1).reshape(P, -1)

    k, rope, slot = shape_constants()
    arrays = {
        "x": np.asarray(x)[0], "w_in": np.asarray(w_in)[0], "w_out": np.asarray(w_out)[0],
        "w_gate": np.asarray(w_gate)[0], "w_up": np.asarray(w_up)[0], "w_down": np.asarray(w_down)[0],
        "b_down": np.asarray(b_down)[0], "router_b": np.asarray(router_b),
        "consts": k, "rope": rope, "slots": slot,
        "cols": np.concatenate([per_partition(norm1_g), per_partition(norm2_g),
                                np.asarray(router_w)[0].reshape(C, P, E).transpose(1, 0, 2).reshape(P, C * E)], axis=1),
        "bias": np.concatenate([per_partition(b_gate), per_partition(b_up)], axis=1),
        "vecs": np.concatenate([np.asarray(a) for a in (a_qnorm_g, a_knorm_g, b_qnorm_g, b_knorm_g, a_lq1, a_lk1,
                                                        a_lq2, a_lk2, a_subln_g)], axis=1),
    }
    arrays = {f"in_{n}": np.ascontiguousarray(a) for n, a in arrays.items()}
    aps = [nc.dram_tensor(n, a.shape, mybir.dt.from_np(a.dtype), kind="ExternalInput").ap() for n, a in arrays.items()]
    out = nc.dram_tensor("out_rows", (ROWS, D), F32, kind="ExternalOutput").ap()
    h2_rows = nc.dram_tensor("h2_rows", (SEQ, D), F32, kind="Internal").ap()
    (x_, w_in_, w_out_, wg_, wu_, wd_, bd_, rb_, k_, rope_, slot_, cols_, bias_, vecs_) = aps
    encoder_layer(nc, x_, w_in_, w_out_, wg_, wu_, wd_, bd_, rb_, k_, rope_, slot_, cols_, bias_, vecs_, out, h2_rows)
    got = _run(nc, [arrays], core_ids=[0]).results[0]["out_rows"]
    return got[:SEQ].reshape(1, SEQ, D)
```

```python
from contextlib import ExitStack

import numpy as np

import concourse.bass as bass
from concourse import mybir

F32 = mybir.dt.float32
F32R = mybir.dt.float32r
BF16 = mybir.dt.bfloat16
I32 = mybir.dt.int32
U32 = mybir.dt.uint32
ALU = mybir.AluOpType
ACT = mybir.ActivationFunctionType
AX = mybir.AxisListType

P = 128
SEQ = 512
D = 1024
T = SEQ // P
C = D // P
HD = 64
NQK = 26
NCH = NQK // 2
VW = 640
WIN = 2304
PAIRS = 8
NU = T * PAIRS
EPS = 1e-6
LAM_INIT = 0.2
SCALE = HD ** -0.5

E = 32
TOPK = 4
SLOTS = 96
OVER = SEQ * TOPK // SLOTS
NB = E + OVER + 3
NX = NB - E
NTHR = (SEQ - 1) // SLOTS
FAR = 4096.0
LIMIT = 7.0
ALPHA = 1.702
HALF = D // 2
UNITS = 2 * C
RING = 4
ROWS = SEQ + SLOTS

K_ID, K_TRI, K_ONE, K_SLOT, K_BIDX, K_E32, K_THR, K_CUM, K_SPARE = (
    0, 128, 256, 384, 480, 480 + NX, 512 + NX, 520 + NX, 584 + NX)
K_HALF = K_SPARE + 1
K_W = K_HALF + 1
C_G1, C_G2, C_RW = 0, C, 2 * C
C_W = C_RW + C * E
V_GAIN, V_LAM, V_SUB = 0, 4 * HD, 8 * HD
V_W = V_SUB + 128


def shape_constants():
    k = np.zeros((P, K_W), np.float32)
    k[:, K_ID:K_ID + P] = np.eye(P)
    k[:, K_TRI:K_TRI + P] = np.triu(np.ones((P, P)), 1)
    k[:, K_ONE:K_ONE + P] = 1.0
    k[:, K_SLOT:K_SLOT + SLOTS] = np.arange(SLOTS) - FAR
    k[:, K_BIDX:K_BIDX + NX] = np.arange(NX)
    k[:, K_E32:K_E32 + E] = np.arange(E)
    k[:, K_THR:K_THR + NTHR] = SLOTS * np.arange(1, NTHR + 1)
    k[:E, K_CUM:K_CUM + E] = np.triu(np.ones((E, E)))
    k[:E, K_CUM + E:K_CUM + 2 * E] = np.eye(E)
    k[:, K_SPARE] = SEQ + np.arange(P)
    k[:, K_HALF] = -0.5

    def freqs(dim):
        return np.float32(10000.0) ** (-(np.arange(0, dim, 2, dtype=np.float32) / np.float32(dim)))

    t = np.arange(SEQ, dtype=np.float32)
    one = t[:, None] * freqs(HD)[None]
    f = freqs(HD // 2)
    two = np.concatenate([(np.arange(SEQ) // 64).astype(np.float32)[:, None] * f,
                          (np.arange(SEQ) % 64).astype(np.float32)[:, None] * f], -1)
    rope = np.zeros((SEQ, 4, HD), np.float32)
    for n, a in enumerate((one, two)):
        a = a.astype(np.float32)
        rope[:, 2 * n] = np.concatenate([np.cos(a), np.cos(a)], -1)
        rope[:, 2 * n + 1] = np.concatenate([np.sin(a), -np.sin(a)], -1)
    rope = rope.reshape(T, P, 4 * HD).transpose(1, 0, 2)
    return k, np.ascontiguousarray(rope)


def encoder_layer(nc, x, w_in, w_out, w_gate, w_up, w_down, b_down, router_b,
                  consts, rope_c, cols_c, bias_c, vecs_c, out, h2_rows):
    with ExitStack() as ctx:
        def sb(name, shape, dt=F32):
            return ctx.enter_context(nc.sbuf_tensor(name, shape, dt))

        def sem(name):
            return ctx.enter_context(nc.semaphore(name))

        bank = [ctx.enter_context(nc.psum_tensor(f"bank{i}", [P, 512], F32)) for i in range(8)]

        W = sb("weights", [P, 3 * C * D])
        w_in_sb = W[:, 0:C * WIN].rearrange("p (c n) -> p c n", c=C)
        wg = W[:, 0:C * D].rearrange("p (c n) -> p c n", c=C)
        wu = W[:, C * D:2 * C * D].rearrange("p (c n) -> p c n", c=C)
        wd = W[:, 2 * C * D:3 * C * D].rearrange("p (c n) -> p c n", c=C)
        w_out_sb = wd

        xres = sb("xres", [P, T, D])
        region2 = sb("region2", [P, T * D])
        xT = region2[:, :].rearrange("p (c s) -> p c s", c=C)
        o_nat = region2[:, :].rearrange("p (t d) -> p t d", t=T)
        w_in_end = C * WIN
        qk_own = sb("qk", [P, NQK * HD])
        qk = [qk_own[:, :], W[:, w_in_end:w_in_end + NQK * HD]]
        qk = [q.rearrange("p (n d) -> p n d", n=NQK) for q in qk]
        bd = qk_own[0:E, 5 * T * E:5 * T * E + D]
        h2T = W[:, 8 * D:9 * D].rearrange("p (c s) -> p c s", c=C)
        oT = W[:, 9 * D:11 * D].rearrange("p (b c s) -> p b c s", b=2, c=C)
        GT = sb("GT", [E, P])
        region4 = sb("region4", [P, NCH * SEQ])
        qkT = region4[:, :].rearrange("p (n s) -> p n s", n=NCH)
        t1, t2 = (W[:, w_in_end + i * NQK * HD:w_in_end + (i + 1) * NQK * HD].rearrange("p (n d) -> p n d", n=NQK)
                  for i in (1, 2))
        xsq = W[:, w_in_end + NQK * HD:w_in_end + NQK * HD + D]
        rope = W[:, w_in_end + 3 * NQK * HD:w_in_end + 3 * NQK * HD + T * 4 * HD].rearrange("p (t n) -> p t n", t=T)
        prob = W[:, 11 * D:14 * D].rearrange("p (b m k) -> p b m k", b=3, m=2)
        probT = W[:, 14 * D:16 * D].rearrange("p (b m j q) -> p b m j q", b=2, m=2, j=4)
        CS = C * SLOTS
        gact, uact, sig, mid = (region2[:, i * CS:(i + 1) * CS].rearrange("p (c s) -> p c s", c=C) for i in range(4))
        xrow = region2[:, 4 * CS:4 * CS + D]
        taken = [0]

        def late(n, parts=P):
            taken[0] += n
            assert taken[0] <= NCH * SEQ
            return region4[0:parts, taken[0] - n:taken[0]]

        xu = late(CS).rearrange("p (c s) -> p c s", c=C)
        bias = late(2 * C * E)
        le = late(NX * E).rearrange("p (j e) -> p j e", j=NX)
        slot_b = late(SLOTS)
        nbc = late(P, E)
        cum = late(2 * E)
        tab_e = late(NB)
        tab_base = late(NB)
        gtab = late(NB, SLOTS)
        stab = late(NB, SLOTS)
        bgc, buc, cnt = late(C), late(C), late(16, E)
        btab = late(4 * NX).rearrange("p (k j) -> p k j", k=4)
        V = sb("V", [P, T, VW])
        v_flat = V[:, :, :].rearrange("p t n -> p (t n)")
        y_sb = v_flat[:, 0:D]
        xg = v_flat[:, D:D + CS].rearrange("p (c s) -> p c s", c=C)
        w_hi = sb("w_hi", [P, RING, HALF], F32R)
        w_lo = sb("w_lo", [P, RING, HALF], F32R)
        mid_hi = sb("mid_hi", [P, C, SLOTS], F32R)
        mid_lo = sb("mid_lo", [P, C, SLOTS], F32R)
        K = sb("K", [P, K_W])
        ropeg = sb("ropeg", [P, 8, HD])
        sq = ropeg[:, :, :].rearrange("p n d -> p (n d)")
        cols = sb("cols", [P, C_W])
        vecs = sb("vecs", [P, V_W])
        rb = sb("rb", [1, E])
        st = sb("st", [P, 64])
        ssq = sb("ssq", [P, NQK])
        rsq = sb("rsq", [P, NQK])
        mx = sb("mx", [P, 4, 2])
        nmx = sb("nmx", [P, 4, 2])
        rs = sb("rs", [P, 4, 2])
        rr = sb("rr", [P, 4, 2])
        nla = sb("nla", [P, 4])
        sub = sb("sub", [P, 8])
        subg = sb("subg", [P, 128])
        lg = sb("lg", [P, E])
        v8 = sb("v8", [P, 8])
        i8 = sb("i8", [P, 8], U32)
        i8f = sb("i8f", [P, 8])
        e4 = sb("e4", [P, 8])
        g4 = sb("g4", [P, 4])
        G, M, pos, oh4, ohg = (qk_own[:, i * T * E:(i + 1) * T * E].rearrange("p (t e) -> p t e", t=T) for i in range(5))
        Grest = sb("Grest", [P, 2, E])
        R = sb("R", [P, T, E, 6], BF16)
        Rcur = sb("Rcur", [P, T, 6], BF16)
        onehot = sb("onehot", [P, T, SLOTS], BF16)
        tab_ei = sb("tab_ei", [P, NB], I32)
        further = sb("further", [P, 1], I32)
        si = sb("si", [SLOTS, 8])
        gidx = sb("gidx", [SLOTS, 1], I32)
        sidx = sb("sidx", [SLOTS, 1], I32)
        gnow = sb("gnow", [SLOTS, 1])

        ident = K[:, K_ID:K_ID + P]
        gain = vecs[:, V_GAIN:V_GAIN + 4 * HD].rearrange("p (n d) -> p n d", n=4)
        lamv = vecs[:, V_LAM:V_LAM + 4 * HD].rearrange("p (n d) -> p n d", n=4)
        bgate = bias[:, 0:C * E].rearrange("p (c e) -> p c e", c=C)
        bup = bias[:, C * E:2 * C * E].rearrange("p (c e) -> p c e", c=C)
        rw = cols[:, C_RW:C_RW + C * E].rearrange("p (c e) -> p c e", c=C)

        x_in = [sem(f"x_in{t}") for t in range(T)]
        K_in, cols_in, const_in = sem("K_in"), sem("cols_in"), sem("const_in")
        win_in = [sem(f"win_in{c}") for c in range(C)]
        wout_in, bd_in, bias_in = sem("wout_in"), sem("bd_in"), sem("bias_in")
        wg_in = [sem(f"wg_in{j}") for j in range(C // 2)]
        wu_in = [sem(f"wu_in{j}") for j in range(C // 2)]
        wd_in = [sem(f"wd_in{j}") for j in range(C // 2)]
        dve_step = sem("dve_step")
        act_step = sem("act_step")
        lam_dot, lam_exp, lam_ready = sem("lam_dot"), sem("lam_exp"), sem("lam_ready")
        xss, mean_ready, root_ready = sem("xss"), sem("mean_ready"), sem("root_ready")
        xT_tr, xT_ready = sem("xT_tr"), sem("xT_ready")
        proj_done, proj_out = sem("proj_done"), sem("proj_out")
        qk_sq, qk_rope, qkT_tr, qkT_ready = sem("qk_sq"), sem("qk_rope"), sem("qkT_tr"), sem("qkT_ready")
        sc_done, max_ready, exp_done, comb_done, rcp_done = (
            sem("sc_done"), sem("max_ready"), sem("exp_done"), sem("comb_done"), sem("rcp_done"))
        pT_tr, pT_act, pT_dve, pv_done, oA_out, oB_out, o_ready = (
            sem("pT_tr"), sem("pT_act"), sem("pT_dve"), sem("pv_done"), sem("oA_out"), sem("oB_out"), sem("o_ready"))
        oT_tr, oT_ready, op_done, res_ready = sem("oT_tr"), sem("oT_ready"), sem("op_done"), sem("res_ready")
        opA_done = sem("opA_done")
        x1_ss, h2_ready, h2T_tr, h2T_ready = sem("x1_ss"), sem("h2_ready"), sem("h2T_tr"), sem("h2T_ready")
        h2_stored = sem("h2_stored")
        lg_done, lg_read, nv_ready, e4_ready, route_ready = (
            sem("lg_done"), sem("lg_read"), sem("nv_ready"), sem("e4_ready"), sem("route_ready"))
        rank_done, pos_ready, GT_tr, GT_ready, bd_done, acc_ready, acc_stored = (
            sem("rank_done"), sem("pos_ready"), sem("GT_tr"), sem("GT_ready"), sem("bd_done"), sem("acc_ready"),
            sem("acc_stored"))
        cnt_done, nbc_ready, cum_done, table_ready = (
            sem("cnt_done"), sem("nbc_ready"), sem("cum_done"), sem("table_ready"))
        zero_ready = sem("zero_ready")
        idx_step, hot_ready, slot_done, gidx_ready, gathered = (
            sem("idx_step"), sem("hot_ready"), sem("slot_done"), sem("gidx_ready"), sem("gathered"))
        xr_tr, xg_ready, xu_ready = sem("xr_tr"), sem("xg_ready"), sem("xu_ready")
        gate_used, up_used, down_used = sem("gate_used"), sem("up_used"), sem("down_used")
        g_step, g_ready, sig_ready, u_step, mid_ready = (
            sem("g_step"), sem("g_ready"), sem("sig_ready"), sem("u_step"), sem("mid_ready"))
        hi_ready, lo_ready, mid_hi_ready, mid_lo_ready = (
            sem("hi_ready"), sem("lo_ready"), sem("mid_hi_ready"), sem("mid_lo_ready"))
        blank = sem("blank")
        pool_turn = sem("pool_turn")
        g_read, u_read, now_ready, y_ready, scattered = (
            sem("g_read"), sem("u_read"), sem("now_ready"), sem("y_ready"), sem("scattered"))

        NCONST = 3
        ORDER = [(t, g) for t in range(T) for g in ((0, 1, 3, 4, 2) if t < T - 2 else (0, 1, 3, 4))] + [(T - 2, 2), (T - 1, 2)]

        def before(t, g):
            return max(i + 1 for i, (_, h) in enumerate(ORDER[:ORDER.index((t, g))]) if h == g)

        EARLY = {2: 1, 5: 5, 7: 8}
        LATE = {1: 0, 2: 2, 3: 3, 4: 4, 5: 6, 6: 7, 7: 9}
        NEXT = {0: 10, 1: 11}
        STEPS = 12
        TAIL = [(T - 2, 10), (T - 2, 11), (T - 1, 1), (T - 1, 3), (T - 1, 4), (T - 1, 5), (T - 1, 6)]

        def steps_beside(n, late):
            t, p = divmod(n, PAIRS)
            if n == NU - 2:
                return [(T - 2, 7), (T - 1, 2)] if late else [(T - 1, 0)]
            if late:
                return [(t - 1, LATE[p])] if t >= 1 and p in LATE else []
            last = [(t - 2, NEXT[p])] if t >= 2 and p in NEXT else []
            return last + ([(t - 1, EARLY[p])] if t >= 1 and p in EARLY else [])

        def h2_bank(t, k):
            return bank[7] if t < T - 1 or k == 4 else bank[3]

        def bd_bank(t, k):
            return bank[7] if t < T - 1 else bank[2 + k - 10]

        h2_dram = h2_rows
        block = ctx.enter_context(nc.Block())

        def psum_pair(b, n):
            return [bank[b + i][:, 0:4 * n].rearrange("p (c s) -> p c s", c=4) for i in range(2)]

        gate_ps, up_ps, xt_ps = psum_pair(0, SLOTS), psum_pair(2, SLOTS), psum_pair(6, SLOTS)
        y_ps = [bank[4], bank[5]]
        slot_ps = bank[6][0:SLOTS, 4 * SLOTS:4 * SLOTS + 6]

        @block.sync
        def _(sp):
            def x_load(t):
                sp.dma_start(xres[:, t, :], x[t * P:(t + 1) * P, :]).then_inc(x_in[t], 16)

            x_load(0)
            sp.dma_start(K[:, :], consts).then_inc(K_in, 16)
            sp.dma_start(cols[:, :], cols_c).then_inc(cols_in, 16)
            for c in range(C):
                sp.dma_start(w_in_sb[:, c, :], w_in[c * P:(c + 1) * P, :]).then_inc(win_in[c], 16)
                if 1 <= c < T:
                    x_load(c)
            sp.dma_start(rope, rope_c).then_inc(const_in, 16)
            sp.dma_start(vecs[:, :], vecs_c.to_broadcast((P, V_W))).then_inc(const_in, 16)
            sp.dma_start(rb[:, :], router_b).then_inc(const_in, 16)

            def load(dst, src, e, j, arrived):
                s = src[e, 2 * j * P:(2 * j + 2) * P, :] if isinstance(e, int) else \
                    src[bass.ds(e, 1), 2 * j * P:(2 * j + 2) * P, :].rearrange("a r n -> (a r) n")
                sp.dma_start(dst[:, 2 * j:2 * j + 2, :], s.rearrange("(c p) n -> p c n", p=P)).then_inc(arrived[j], 16)

            sp.wait_ge(proj_done, 5 * T)
            for j in range(C // 2):
                load(wg, w_gate, 0, j, wg_in)
            sp.wait_ge(qk_rope, T)
            sp.wait_ge(qkT_tr, 4 * T)
            sp.dma_start(w_out_sb, w_out.rearrange("(c p) n -> p c n", p=P)).then_inc(wout_in, 16)
            sp.dma_start(bd, b_down).then_inc(bd_in, 16)
            sp.wait_ge(pv_done, NU)
            sp.dma_start(bias, bias_c).then_inc(bias_in, 16)
            for j in (2, 3):
                load(wu, w_up, 0, j, wu_in)
            sp.wait_ge(opA_done, 1)
            for j in (0, 1):
                load(wd, w_down, 0, j, wd_in)
            sp.wait_ge(op_done, 2 * T)
            load(wu, w_up, 0, 1, wu_in)
            for j in (2, 3):
                load(wd, w_down, 0, j, wd_in)
            sp.wait_ge(lg_done, T)
            load(wu, w_up, 0, 0, wu_in)

            def gate_in(b, e):
                for j in range(C // 2):
                    sp.wait_ge(gate_used, (b - 1) * C + 2 * j + 2)
                    load(wg, w_gate, e, j, wg_in)

            def up_in(b, e):
                for j in range(C // 2):
                    sp.wait_ge(up_used, (b - 1) * C + 2 * j + 2)
                    load(wu, w_up, e, j, wu_in)

            def down_in(b, e):
                for j in range(C // 2):
                    sp.wait_ge(lo_ready, (b - 1) * UNITS + RING * j + RING)
                    load(wd, w_down, e, j, wd_in)

            gate_in(1, 1)
            up_in(1, 1)
            sp.wait_ge(table_ready, 1)
            n = sp.value_load(further[0:1, 0:1], min_val=0, max_val=OVER) + E
            with sp.Fori(1, n - 1) as i:
                e_now = sp.value_load(tab_ei[0:1, bass.ds(i, 1)], min_val=0, max_val=E - 1)
                e_next = sp.value_load(tab_ei[0:1, bass.ds(i + 1, 1)], min_val=0, max_val=E - 1)
                gate_in(i + 1, e_next)
                down_in(i, e_now)
                up_in(i + 1, e_next)
            e_last = sp.value_load(tab_ei[0:1, bass.ds(n - 1, 1)], min_val=0, max_val=E - 1)
            down_in(n - 1, e_last)

        @block.tensor
        def _(pe):
            mm, tr = nc.tensor.matmul, nc.tensor.transpose

            def keep_warm(n, to=bank[5], of=K):
                for _ in range(n):
                    mm(to[:, :], of[:, 0:P], of[:, 0:512], start=True, stop=True)

            pe.wait_ge(blank, 1)
            keep_warm(2, bank[0], W[:, w_in_end:w_in_end + 512])
            pe.wait_ge(K_in, 16)

            def x_transposes(t):
                pe.wait_ge(x_in[t], 16)
                for u in (2 * t, 2 * t + 1):
                    if u >= 3:
                        pe.wait_ge(xT_ready, u - 2)
                    for j in range(4):
                        c = 4 * (u % 2) + j
                        last = tr(bank[5 + u % 3][:, j * P:(j + 1) * P], xres[:, t, c * P:(c + 1) * P], ident)
                    last.then_inc(xT_tr, 1)

            x_transposes(0)
            keep_warm(2, bank[0])

            def proj(t, g, c):
                n0, n1 = 512 * g, min(512 * g + 512, WIN)
                last = mm(bank[g][:, 0:n1 - n0], xT[:, c, t * P:(t + 1) * P], w_in_sb[:, c, n0:n1],
                          start=(c == 0), stop=(c == C - 1))
                if c == C - 1:
                    last.then_inc(proj_done, 1)

            def qk_transposes(t):
                pe.wait_ge(qk_rope, t + 1)
                for k in range(4):
                    w = 4 * t + k
                    pe.wait_ge(xT_ready, 2 * T)
                    if w >= 3:
                        pe.wait_ge(qkT_ready, w - 2)
                    for j in range(4 * k, min(4 * k + 4, NCH)):
                        last = tr(bank[5 + w % 3][:, (j % 4) * P:(j % 4 + 1) * P],
                                  qk[t % 2][:, 2 * j:2 * j + 2, :].rearrange("p a d -> p (a d)"), ident)
                    last.then_inc(qkT_tr, 1)

            for c in range(C):
                pe.wait_ge(win_in[c], 16)
                pe.wait_ge(xT_ready, 1 + c // 4)
                for _, g in ORDER[:5]:
                    proj(0, g, c)
                if 2 <= c < T + 1:
                    x_transposes(c - 1)
            for t, g in ORDER[5:]:
                pe.wait_ge(xT_ready, 2 * t + 2)
                pe.wait_ge(proj_out, before(t, g))
                for c in range(C):
                    proj(t, g, c)
                if (t, g) in ((1, 2), (T - 2, 4), (T - 1, 4)):
                    qk_transposes(t - 1)
            qk_transposes(T - 1)

            def scores(n):
                qt, p = divmod(n, PAIRS)
                if n >= 2:
                    pe.wait_ge(exp_done, 2 * n - 2)
                kc = 4 + p if p < 4 else 12
                qc = p if p < 4 else 8 + p - 4
                for m in range(2):
                    r = slice(HD * m, HD * m + HD)
                    last = mm(bank[2 * (n % 2) + m][:, :], qkT[r, qc, qt * P:(qt + 1) * P], qkT[r, kc, :],
                              start=True, stop=True)
                last.then_inc(sc_done, 1)

            def p_transposes(n):
                qt, p = divmod(n, PAIRS)
                if n >= 1:
                    pe.wait_ge(pT_act, n)
                if p < 4:
                    if qt >= 1:
                        pe.wait_ge(pT_dve, 4 * qt)
                    pe.wait_ge(comb_done, 4 * qt + p + 1)
                else:
                    pe.wait_ge(exp_done, 2 * n + 2)
                    if n % PAIRS >= 5 or qt >= 1:
                        pe.wait_ge(pT_dve, 4 * qt + p - 4)
                for m in range(1 if p < 4 else 2):
                    for j in range(4):
                        last = tr(bank[4 + m][:, j * P:(j + 1) * P], prob[:, n % 3, m, j * P:(j + 1) * P], ident)
                last.then_inc(pT_tr, 1)

            def pv(n):
                qt, p = divmod(n, PAIRS)
                pe.wait_ge(pT_act, n + 1)
                o = bank[6][:, (n % 4) * P:(n % 4 + 1) * P]
                if p < 4:
                    if p >= 1:
                        pe.wait_ge(oA_out, 4 * qt + p)
                    elif qt >= 1:
                        pe.wait_ge(oB_out, 4 * qt)
                    for j in range(4):
                        last = mm(o, probT[:, n % 2, 0, j, :], V[:, j, p * P:(p + 1) * P], start=(j == 0), stop=(j == 3))
                else:
                    pe.wait_ge(pT_dve, 4 * qt + p - 3)
                    if p == 4:
                        pe.wait_ge(oA_out, 4 * qt + 4)
                    else:
                        pe.wait_ge(oB_out, 4 * qt + p - 4)
                    for m in range(2):
                        for j in range(4):
                            last = mm(o[:, m * HD:(m + 1) * HD], probT[:, n % 2, m, j, :],
                                      V[:, j, 512 + m * HD:512 + (m + 1) * HD], start=(j == 0), stop=(j == 3))
                last.then_inc(pv_done, 1)

            def after(t, k):
                b7 = bank[7]
                if k == 0:
                    pe.wait_ge(o_ready, 2 * t + 1)
                    if t == 0:
                        pe.wait_ge(qkT_ready, 4 * T)
                    elif t < T - 1:
                        pe.wait_ge(acc_ready, 2 * t)
                    else:
                        pe.wait_ge(nv_ready, t)
                elif k == 1:
                    pe.wait_ge(o_ready, 2 * t + 2)
                    if t == T - 1:
                        pe.wait_ge(acc_ready, 2 * t)
                    pe.wait_ge(oT_ready, 2 * t + 1)
                if k < 2:
                    for j in range(4):
                        last = tr(b7[:, j * P:(j + 1) * P], o_nat[:, t, (4 * k + j) * P:(4 * k + j + 1) * P], ident)
                    last.then_inc(oT_tr, 1)
                elif k < 4 and t == T - 1:
                    pe.wait_ge(oT_ready, 2 * t + k - 1)
                    for h in range(2):
                        for c in range(4 * (k - 2), 4 * (k - 2) + 4):
                            last = mm(bank[h][:, :], oT[:, t % 2, c, :], w_out_sb[:, c, h * 512:(h + 1) * 512],
                                      start=(c == 0), stop=(c == C - 1))
                        if k == 3:
                            last.then_inc(op_done, 1)
                    if k == 2:
                        last.then_inc(opA_done, 1)
                elif k < 4:
                    pe.wait_ge(oT_ready, 2 * t + 2)
                    pe.wait_ge(wout_in, 16)
                    if k == 3:
                        pe.wait_ge(res_ready, 2 * t + 1)
                    for c in range(C):
                        last = mm(b7[:, :], oT[:, t % 2, c, :], w_out_sb[:, c, (k - 2) * 512:(k - 1) * 512],
                                  start=(c == 0), stop=(c == C - 1))
                    last.then_inc(op_done, 1)
                elif k < 6:
                    pe.wait_ge(h2_ready, t + 1)
                    if k == 4:
                        pe.wait_ge(res_ready, 2 * t + 2)
                    elif t < T - 1:
                        pe.wait_ge(h2T_ready, 2 * t + 1)
                    for j in range(4):
                        last = tr(h2_bank(t, k)[:, j * P:(j + 1) * P], o_nat[:, t, (4 * (k - 4) + j) * P:(4 * (k - 4) + j + 1) * P], ident)
                    last.then_inc(h2T_tr, 1)
                elif k == 6:
                    pe.wait_ge(h2T_ready, 2 * t + 2)
                    for c in range(C):
                        mm(b7[:, 0:E], h2T[:, c, :], rw[:, c, :], start=(c == 0), stop=False)
                    pe.wait_ge(const_in, 16 * NCONST)
                    mm(b7[:, 0:E], K[0:1, K_ONE:K_ONE + P], rb[:, :], start=False, stop=True).then_inc(lg_done, 1)
                elif k == 7:
                    pass
                elif k == 8:
                    pe.wait_ge(nv_ready, t + 1)
                    for s in range(t):
                        mm(b7[:, 0:E], K[:, K_ONE:K_ONE + P], M[:, s, :], start=(s == 0), stop=False)
                    pe.wait_ge(route_ready, t + 1)
                    mm(b7[:, 0:E], K[:, K_TRI:K_TRI + P], M[:, t, :], start=(t == 0), stop=True).then_inc(rank_done, 1)
                elif k == 9:
                    pe.wait_ge(pos_ready, t + 1)
                    tr(b7[0:E, P:2 * P], G[:, t, :], ident).then_inc(GT_tr, 1)
                else:
                    pe.wait_ge(GT_ready, t + 1)
                    pe.wait_ge(bd_in, 16)
                    if k == 11 and t < T - 1:
                        pe.wait_ge(acc_ready, 2 * t + 1)
                    mm(bd_bank(t, k)[:, :], GT[:, :], bd[:, (k - 10) * 512:(k - 9) * 512], start=True, stop=True).then_inc(bd_done, 1)

            pe.wait_ge(qkT_ready, 4 * T)
            pe.wait_ge(proj_out, 5 * T)
            scores(0)
            scores(1)
            for n in range(NU):
                if n + 2 < NU:
                    scores(n + 2)
                for t, k in steps_beside(n, False):
                    after(t, k)
                p_transposes(n)
                if n >= 1:
                    pv(n - 1)
                for t, k in steps_beside(n, True):
                    after(t, k)
            pv(NU - 1)
            for t, k in TAIL:
                after(t, k)
                keep_warm({1: 1, 3: 3, 6: 1}.get(k, 0))
            after(T - 1, 8)
            keep_warm(1)

            for t in range(T):
                last = mm(bank[4][0:E, 0:1], M[:, t, :], K[:, K_ONE:K_ONE + 1], start=(t == 0), stop=(t == T - 1))
            last.then_inc(cnt_done, 1)

            def slot_sums(b):
                pe.wait_ge(hot_ready, b + 1)
                if not isinstance(b, int) or b > 0:
                    pe.wait_ge(gidx_ready, b)
                for t in range(T):
                    last = mm(slot_ps, onehot[:, t, :], Rcur[:, t, :], start=(t == 0), stop=(t == T - 1))
                last.then_inc(slot_done, 1)

            def row_transposes(b):
                pe.wait_ge(gathered, 16 * (b + 1))
                if not isinstance(b, int) or b > 0:
                    pe.wait_ge(xg_ready, b)
                for c in range(C):
                    last = tr(xt_ps[c // 4][:, c % 4, :], xrow[0:SLOTS, c * P:(c + 1) * P], ident[0:SLOTS, 0:SLOTS])
                last.then_inc(xr_tr, 1)

            def product(w, arrived, xt, ps, used, b):
                for c in range(C):
                    if c % 2 == 0:
                        pe.wait_ge(arrived[c // 2], 16 * (b + 1))
                    for f in range(C):
                        last = mm(ps[f // 4][:, f % 4, :], w[:, c, f * P:(f + 1) * P], xt[:, c, :],
                                  start=(c == 0 and f % 4 == 0), stop=(c == C - 1), skip_group_check=True)
                    last.then_inc(used, 1)

            def gate(b):
                pe.wait_ge(xg_ready, b + 1)
                if not isinstance(b, int) or b > 0:
                    pe.wait_ge(g_read, b)
                product(wg, wg_in, xg, gate_ps, gate_used, b)

            def up(b):
                pe.wait_ge(xu_ready, b + 1)
                if isinstance(b, int) and b == 0:
                    pe.wait_ge(acc_ready, 2 * T)
                else:
                    pe.wait_ge(u_read, b)
                product(wu, wu_in, xu, up_ps, up_used, b)

            def down(b):
                pe.wait_ge(mid_lo_ready, b + 1)
                if not isinstance(b, int) or b > 0:
                    pe.wait_ge(y_ready, b)
                for u in range(UNITS):
                    c, h = divmod(u, 2)
                    y = y_ps[h][0:SLOTS, :]
                    pe.wait_ge(lo_ready, UNITS * b + u + 1)
                    mm(y, mid_hi[:, c, :], w_hi[:, u % RING, :], start=(c == 0), stop=False)
                    mm(y, mid_hi[:, c, :], w_lo[:, u % RING, :], start=False, stop=False)
                    mm(y, mid_lo[:, c, :], w_hi[:, u % RING, :], start=False, stop=(c == C - 1)).then_inc(down_used, 1)

            slot_sums(0)
            keep_warm(2)
            pe.wait_ge(nbc_ready, 1)
            mm(bank[4][:, 0:2 * E], nbc[:, :], K[0:E, K_CUM:K_CUM + 2 * E], start=True, stop=True).then_inc(cum_done, 1)
            after(T - 1, 9)
            pe.wait_ge(GT_ready, T)
            keep_warm(2)
            row_transposes(0)
            slot_sums(1)
            for k in (10, 11):
                after(T - 1, k)
            gate(0)
            row_transposes(1)
            slot_sums(2)
            up(0)
            pe.wait_ge(table_ready, 1)
            n_blocks = pe.value_load(further[0:1, 0:1], min_val=0, max_val=OVER) + E
            with pe.Fori(0, n_blocks - 1) as i:
                gate(i + 1)
                row_transposes(i + 2)
                slot_sums(i + 3)
                down(i)
                up(i + 1)
            down(n_blocks - 1)

        @block.scalar
        def _(act):
            A = nc.scalar.activation
            steps = [0]

            def link(ins):
                steps[0] += 1
                ins.then_inc(act_step, 1)
                act.wait_ge(act_step, steps[0])

            for t in range(T):
                act.wait_ge(x_in[t], 16)
                if t:
                    act.wait_ge(xss, t)
                A(xsq, xres[:, t, :], ACT.Square, accum_out=st[:, t:t + 1]).then_inc(xss, 1)
            act.wait_ge(lam_dot, 1)
            A(st[:, 10:12], st[:, 8:10], ACT.Exp).then_inc(lam_exp, 1)

            def proj_evacuate(t, g):
                b, r1 = t % 2, st[:, 4 + t:5 + t]
                if g == 0 and t >= 2:
                    act.wait_ge(qkT_tr, 4 * (t - 1))
                act.wait_ge(proj_done, ORDER.index((t, g)) + 1)
                if g < 2:
                    A(qk[b][:, 8 * g:8 * g + 8, :].rearrange("p n d -> p (n d)"), bank[g][:, :], ACT.Copy,
                      scale=r1).then_inc(proj_out, 1)
                elif g == 2:
                    A(V[:, t, 0:512], bank[g][:, :], ACT.Copy, scale=r1).then_inc(proj_out, 1)
                elif g == 3:
                    A(qk[b][:, 16:24, :].rearrange("p (j g) d -> p g j d", g=2),
                      bank[g][:, :].rearrange("p (g j d) -> p g j d", g=2, j=4), ACT.Copy,
                      scale=r1).then_inc(proj_out, 1)
                else:
                    link(A(qk[b][:, 24:26, :].rearrange("p n d -> p (n d)"), bank[g][:, 0:128], ACT.Copy, scale=r1))
                    A(V[:, t, 512:640], bank[g][:, 128:256], ACT.Copy, scale=r1).then_inc(proj_out, 1)
                    if t:
                        act.wait_ge(qk_rope, t)
                    act.wait_ge(proj_out, ORDER.index((t, g)) + 1)
                    A(t1, qk[b], ACT.Square).then_inc(qk_sq, 1)

            def qkT_evacuate(t):
                for k in range(4):
                    act.wait_ge(qkT_tr, 4 * t + k + 1)
                    n = min(4, NCH - 4 * k)
                    A(qkT[:, 4 * k:4 * k + n, t * P:(t + 1) * P],
                      bank[5 + (4 * t + k) % 3][:, 0:n * P].rearrange("p (j s) -> p j s", j=n), ACT.Copy).then_inc(qkT_ready, 1)

            act.wait_ge(root_ready, 1)
            for t, g in ORDER:
                proj_evacuate(t, g)
                if (t, g) in ((1, 2), (T - 2, 4), (T - 1, 4)):
                    qkT_evacuate(t - 1)
            qkT_evacuate(T - 1)

            def exps(n):
                act.wait_ge(max_ready, n + 1)
                if n >= 3:
                    act.wait_ge(pT_tr, n - 2)
                if n >= 4:
                    act.wait_ge(rcp_done, n - 3)
                for m in range(2):
                    A(prob[:, n % 3, m, :], bank[2 * (n % 2) + m][:, :], ACT.Exp, bias=nmx[:, n % 4, m:m + 1],
                      scale=SCALE, accum_out=rs[:, n % 4, m:m + 1]).then_inc(exp_done, 1)

            def pT_evacuate(n):
                act.wait_ge(pT_tr, n + 1)
                if n >= 2:
                    act.wait_ge(pv_done, n - 1)
                A(probT[:, n % 2, 0, :, :].rearrange("p j q -> p (j q)"), bank[4][:, :], ACT.Copy).then_inc(pT_act, 1)

            def oA_evacuate(n):
                qt, p = divmod(n, PAIRS)
                if p < 4:
                    act.wait_ge(pv_done, n + 1)
                    A(o_nat[:, qt, p * P:(p + 1) * P], bank[6][:, (n % 4) * P:(n % 4 + 1) * P], ACT.Copy).then_inc(oA_out, 1)

            def after(t, k):
                if k < 2:
                    act.wait_ge(oT_tr, 2 * t + k + 1)
                    if t >= 2 and k == 0:
                        act.wait_ge(op_done, 2 * (t - 1))
                    A(oT[:, t % 2, 4 * k:4 * k + 4, :].rearrange("p c s -> p (c s)"), bank[7][:, :], ACT.Copy).then_inc(oT_ready, 1)
                elif k == 3:
                    act.wait_ge(res_ready, 2 * t + 2)
                    if t:
                        act.wait_ge(lg_done, t)
                    A(h2T.rearrange("p c s -> p (c s)"), xres[:, t, :], ACT.Square, accum_out=st[:, 16 + t:17 + t]).then_inc(x1_ss, 1)
                elif k == 6:
                    act.wait_ge(nv_ready, t + 1)
                    A(e4[:, 0:4], v8[:, 0:4], ACT.Exp, bias=e4[:, 4:5], accum_out=e4[:, 5:6]).then_inc(e4_ready, 1)
                elif k == 9:
                    act.wait_ge(GT_tr, t + 1)
                    if t:
                        act.wait_ge(bd_done, 2 * t)
                    A(GT[:, :], bank[7][0:E, P:2 * P], ACT.Copy).then_inc(GT_ready, 1)

            exps(0)
            exps(1)
            for n in range(NU):
                if n + 2 < NU:
                    exps(n + 2)
                for t, k in steps_beside(n, False):
                    after(t, k)
                pT_evacuate(n)
                if n >= 1:
                    oA_evacuate(n - 1)
                for t, k in steps_beside(n, True):
                    after(t, k)
            for t, k in TAIL:
                after(t, k)
            for k in range(7, STEPS):
                after(T - 1, k)

            def copy_xT(b):
                act.wait_ge(xg_ready, b + 1)
                if not isinstance(b, int) or b > 0:
                    act.wait_ge(up_used, C * b)
                A(xu, xg, ACT.Copy).then_inc(xu_ready, 1)

            def sigmoid(b):
                act.wait_ge(g_ready, b + 1)
                A(sig, gact, ACT.Sigmoid, scale=ALPHA).then_inc(sig_ready, 1)

            def high_parts(b, u0, u1):
                for u in range(u0, u1):
                    c, h = divmod(u, 2)
                    if u % RING == 0:
                        act.wait_ge(wd_in[u // RING], 16 * (b + 1))
                    if not isinstance(b, int) or b > 0 or u >= RING:
                        act.wait_ge(down_used, UNITS * b + u + 1 - RING)
                    A(w_hi[:, u % RING, :], wd[:, c, h * HALF:(h + 1) * HALF], ACT.Copy).then_inc(hi_ready, 1)

            def mid_high(b):
                act.wait_ge(mid_ready, b + 1)
                if not isinstance(b, int) or b > 0:
                    act.wait_ge(down_used, UNITS * b)
                A(mid_hi[:, :, :], mid, ACT.Copy).then_inc(mid_hi_ready, 1)

            def rows_out(b):
                act.wait_ge(down_used, UNITS * (b + 1))
                act.wait_ge(now_ready, b + 1)
                if isinstance(b, int) and b == 0:
                    act.wait_ge(acc_stored, 16 * (T + 1))
                else:
                    act.wait_ge(scattered, 16 * b)
                A(y_sb[0:SLOTS, 0:512], y_ps[0][0:SLOTS, :], ACT.Copy, scale=gnow[:, 0:1])
                A(y_sb[0:SLOTS, 512:D], y_ps[1][0:SLOTS, :], ACT.Copy, scale=gnow[:, 0:1]).then_inc(y_ready, 1)

            copy_xT(0)
            sigmoid(0)
            copy_xT(1)
            mid_high(0)
            high_parts(0, 0, RING)
            act.wait_ge(table_ready, 1)
            n_blocks = act.value_load(further[0:1, 0:1], min_val=0, max_val=OVER) + E
            with act.Fori(0, n_blocks - 1) as i:
                high_parts(i, RING, UNITS)
                rows_out(i)
                sigmoid(i + 1)
                copy_xT(i + 2)
                mid_high(i + 1)
                high_parts(i + 1, 0, RING)
            high_parts(n_blocks - 1, RING, UNITS)
            rows_out(n_blocks - 1)

        @block.vector
        def _(dve):
            v = nc.vector
            steps = [0]

            def link(ins):
                steps[0] += 1
                ins.then_inc(dve_step, 1)
                dve.wait_ge(dve_step, steps[0])

            asked = [0]

            def mean(out, ss, width):
                asked[0] += 1
                v.tensor_scalar(out, ss, 1.0 / width, EPS, ALU.mult, ALU.add).then_inc(mean_ready, 1)

            def rms(out, ss, width):
                mean(out, ss, width)
                dve.wait_ge(root_ready, asked[0])

            v.memset(W[:, w_in_end:w_in_end + 512], 1.0).then_inc(blank, 1)
            dve.wait_ge(cols_in, 16)
            dve.wait_ge(K_in, 16)
            g1 = cols[:, C_G1:C_G1 + C]
            g2 = cols[:, C_G2:C_G2 + C]
            for u in range(2 * T):
                t, h = divmod(u, 2)
                dve.wait_ge(xT_tr, u + 1)
                v.tensor_tensor(xT[:, 4 * h:4 * h + 4, t * P:(t + 1) * P],
                                bank[5 + u % 3][:, :].rearrange("p (c s) -> p c s", c=4),
                                g1[:, 4 * h:4 * h + 4].unsqueeze(2).to_broadcast((P, 4, P)), ALU.mult).then_inc(xT_ready, 1)
            dve.wait_ge(xss, T)
            rms(st[:, 4:8], st[:, 0:4], D)
            for t in range(T):
                v.tensor_scalar(R[:, t, :, 0], K[:, K_SPARE:K_SPARE + 1].to_broadcast((P, E)), -float(SEQ), None, ALU.add)
                v.memset(R[:, t, :, 1], float(t))
            v.memset(R[:, :, :, 2], 1.0)
            dve.wait_ge(const_in, 16 * NCONST)
            link(v.tensor_tensor(sq[:, 0:HD], lamv[:, 0, :], lamv[:, 1, :], ALU.mult))
            link(v.tensor_tensor(sq[:, HD:2 * HD], lamv[:, 2, :], lamv[:, 3, :], ALU.mult))
            v.tensor_reduce(st[:, 8:10], sq[:, 0:2 * HD].rearrange("p (a d) -> p a d", a=2), AX.X, ALU.add).then_inc(lam_dot, 1)
            dve.wait_ge(lam_exp, 1)
            link(v.tensor_tensor(st[:, 12:13], st[:, 11:12], st[:, 10:11], ALU.subtract))
            link(v.tensor_scalar(st[:, 12:13], st[:, 12:13], -LAM_INIT, None, ALU.add))
            link(v.tensor_scalar(subg[:, :], vecs[:, V_SUB:V_SUB + 128], 1.0 - LAM_INIT, None, ALU.mult))

            kinds = ((0, 8, 0), (8, 16, 0), (16, 24, 1), (24, 26, 1))

            def rotate(t):
                b = t % 2
                n = qk[b]
                for k, (_, _, tab) in enumerate(kinds):
                    for s in range(2):
                        lastk = v.tensor_tensor(ropeg[:, 2 * k + s, :], rope[:, t, (2 * tab + s) * HD:(2 * tab + s + 1) * HD],
                                                gain[:, k, :], ALU.mult)
                link(lastk)
                dve.wait_ge(qk_sq, t + 1)
                link(v.tensor_reduce(ssq[:, :], t1, AX.X, ALU.add))
                rms(rsq[:, :], ssq[:, :], HD)
                link(v.tensor_tensor(n, n, rsq[:, :].unsqueeze(2).to_broadcast((P, NQK, HD)), ALU.mult))
                for k, (lo, hi, _) in enumerate(kinds):
                    for s, dst in ((0, t1), (1, t2)):
                        lastk = v.tensor_tensor(dst[:, lo:hi, :], n[:, lo:hi, :],
                                                ropeg[:, 2 * k + s, :].unsqueeze(1).to_broadcast((P, hi - lo, HD)), ALU.mult)
                link(lastk)
                h = HD // 2
                v.tensor_tensor(n[:, :, 0:h], t1[:, :, 0:h], t2[:, :, h:HD], ALU.add)
                v.tensor_tensor(n[:, :, h:HD], t1[:, :, h:HD], t2[:, :, 0:h], ALU.add).then_inc(qk_rope, 1)

            for t in range(T):
                rotate(t)

            def row_max(n):
                dve.wait_ge(sc_done, n + 1)
                for m in range(2):
                    lastk = v.tensor_reduce(mx[:, n % 4, m:m + 1], bank[2 * (n % 2) + m][:, :], AX.X, ALU.max)
                link(lastk)
                v.tensor_scalar(nmx[:, n % 4, :], mx[:, n % 4, :], -SCALE, None, ALU.mult).then_inc(max_ready, 1)

            def combine(n):
                qt, p = divmod(n, PAIRS)
                dve.wait_ge(exp_done, 2 * n + 2)
                if p >= 4:
                    v.reciprocal(rr[:, n % 4, :], rs[:, n % 4, :]).then_inc(rcp_done, 1)
                    return
                v.reciprocal(rr[:, n % 4, :], rs[:, n % 4, :]).then_inc(rcp_done, 1)
                dve.wait_ge(rcp_done, n + 1)
                v.tensor_tensor(nla[:, n % 4:n % 4 + 1], rr[:, n % 4, 1:2], st[:, 12:13], ALU.mult)
                a, c = prob[:, n % 3, 0, :], prob[:, n % 3, 1, :]
                link(v.tensor_scalar(a, a, rr[:, n % 4, 0:1], None, ALU.mult))
                v.scalar_tensor_tensor(out=a, in0=c, scalar=nla[:, n % 4:n % 4 + 1], in1=a, op0=ALU.mult,
                                       op1=ALU.add).then_inc(comb_done, 1)

            def pT_evacuate(n):
                if n % PAIRS >= 4:
                    dve.wait_ge(pT_tr, n + 1)
                    if n >= 2:
                        dve.wait_ge(pv_done, n - 1)
                    v.tensor_copy(probT[:, n % 2, 1, :, :].rearrange("p j q -> p (j q)"), bank[5][:, :]).then_inc(pT_dve, 1)

            def oB_evacuate(n):
                qt, p = divmod(n, PAIRS)
                if p >= 4:
                    dve.wait_ge(pv_done, n + 1)
                    dve.wait_ge(rcp_done, n + 1)
                    v.tensor_tensor(o_nat[:, qt, 512:1024].rearrange("p (g j d) -> p g j d", g=2, j=4)[:, :, p - 4, :],
                                    bank[6][:, (n % 4) * P:(n % 4 + 1) * P].rearrange("p (m d) -> p m d", m=2),
                                    rr[:, n % 4, :].unsqueeze(2).to_broadcast((P, 2, HD)), ALU.mult).then_inc(oB_out, 1)

            def sub_mean(qt):
                dve.wait_ge(oA_out, 4 * qt + 4)
                o = o_nat[:, qt, 0:512].rearrange("p (h d) -> p h d", h=4)
                s3 = sq.rearrange("p (h d) -> p h d", h=4)
                link(v.tensor_tensor(s3, o, o, ALU.mult))
                link(v.tensor_reduce(sub[:, 0:4], s3, AX.X, ALU.add))
                mean(sub[:, 4:8], sub[:, 0:4], 128)

            def sub_norm(qt):
                dve.wait_ge(root_ready, asked[0])
                o = o_nat[:, qt, 0:512].rearrange("p (h d) -> p h d", h=4)
                link(v.tensor_tensor(o, o, sub[:, 4:8].unsqueeze(2).to_broadcast((P, 4, P)), ALU.mult))
                v.tensor_tensor(o, o, subg[:, :].unsqueeze(1).to_broadcast((P, 4, P)), ALU.mult).then_inc(o_ready, 1)

            def gate_parts(t):
                link(v.tensor_copy(R[:, t, :, 3], G[:, t, :]))
                link(v.tensor_tensor(Grest[:, 0, :], G[:, t, :], R[:, t, :, 3], ALU.subtract))
                link(v.tensor_copy(R[:, t, :, 4], Grest[:, 0, :]))
                link(v.tensor_tensor(Grest[:, 1, :], Grest[:, 0, :], R[:, t, :, 4], ALU.subtract))
                link(v.tensor_copy(R[:, t, :, 5], Grest[:, 1, :]))

            def after(t, k):
                b7 = bank[7]
                if k in (2, 3):
                    if t == T - 1 and k == 2:
                        return
                    for h in (0, 1) if t == T - 1 else (k - 2,):
                        dve.wait_ge(op_done, 2 * t + h + 1)
                        xx = xres[:, t, h * 512:(h + 1) * 512]
                        v.tensor_tensor(xx, (bank[h] if t == T - 1 else b7)[:, :], xx, ALU.add).then_inc(res_ready, 1)
                    if k == 3:
                        dve.wait_ge(x1_ss, t + 1)
                        rms(st[:, 20 + t:21 + t], st[:, 16 + t:17 + t], D)
                        dve.wait_ge(oT_tr, 2 * t + 2)
                        v.tensor_scalar(o_nat[:, t, :], xres[:, t, :], st[:, 20 + t:21 + t], None, ALU.mult).then_inc(h2_ready, 1)
                elif k in (4, 5):
                    h = k - 4
                    dve.wait_ge(h2T_tr, 2 * t + h + 1)
                    if t:
                        dve.wait_ge(lg_done, t)
                    v.tensor_tensor(h2T[:, 4 * h:4 * h + 4, :], h2_bank(t, k)[:, :].rearrange("p (c s) -> p c s", c=4),
                                    g2[:, 4 * h:4 * h + 4].unsqueeze(2).to_broadcast((P, 4, P)), ALU.mult).then_inc(h2T_ready, 1)
                elif k == 6:
                    dve.wait_ge(lg_done, t + 1)
                    link(v.tensor_copy(lg[:, :], b7[:, 0:E]))
                    link(v.max(v8[:, :], lg[:, :]))
                    v.tensor_scalar(e4[:, 4:5], v8[:, 0:1], -1.0, None, ALU.mult).then_inc(nv_ready, 1)
                    link(v.max_index(i8[:, :], v8[:, :], lg[:, :]))
                    link(v.tensor_copy(i8f[:, :], i8[:, :]))
                elif k == 7:
                    link(v.tensor_tensor(oh4[:, :, :], K[:, K_E32:K_E32 + E].unsqueeze(1).to_broadcast((P, 4, E)),
                                         i8f[:, 0:4].unsqueeze(2).to_broadcast((P, 4, E)), ALU.is_equal))
                    v.tensor_reduce(M[:, t, :], oh4[:, :, :].rearrange("p j e -> p e j"), AX.X, ALU.add)
                    dve.wait_ge(e4_ready, t + 1)
                    link(v.reciprocal(e4[:, 6:7], e4[:, 5:6]))
                    link(v.tensor_scalar(g4[:, :], e4[:, 0:4], e4[:, 6:7], None, ALU.mult))
                    link(v.tensor_tensor(ohg[:, :, :], oh4[:, :, :], g4[:, :].unsqueeze(2).to_broadcast((P, 4, E)), ALU.mult))
                    v.tensor_reduce(G[:, t, :], ohg[:, :, :].rearrange("p j e -> p e j"), AX.X, ALU.add).then_inc(route_ready, 1)
                    dve.wait_ge(route_ready, t + 1)
                    if t == T - 1:
                        gate_parts(t)
                elif k == 8:
                    dve.wait_ge(rank_done, t + 1)
                    v.scalar_tensor_tensor(out=pos[:, t, :], in0=M[:, t, :], scalar=-FAR, in1=b7[:, 0:E], op0=ALU.mult,
                                           op1=ALU.add).then_inc(pos_ready, 1)
                elif k in (10, 11):
                    h = k - 10
                    dve.wait_ge(bd_done, 2 * t + h + 1)
                    if h == 0:
                        dve.wait_ge(h2_ready, t + 1)
                    xx = xres[:, t, h * 512:(h + 1) * 512]
                    v.tensor_tensor(xx, bd_bank(t, k)[:, :], xx, ALU.add).then_inc(acc_ready, 1)
                    if k == 11 and t < T - 1:
                        gate_parts(t)

            row_max(0)
            row_max(1)
            combine(0)
            for n in range(NU):
                qt, p = divmod(n, PAIRS)
                if n + 2 < NU:
                    row_max(n + 2)
                if n + 1 < NU:
                    combine(n + 1)
                if p == 6:
                    sub_norm(qt)
                for t, k in steps_beside(n, False):
                    after(t, k)
                pT_evacuate(n)
                if n >= 1:
                    oB_evacuate(n - 1)
                    if (n - 1) % PAIRS == 4:
                        sub_mean(qt)
                    if (n - 1) % PAIRS == PAIRS - 1:
                        dve.wait_ge(oB_out, 4 * qt)
                        v.tensor_copy(sub[:, 0:1], sub[:, 4:5]).then_inc(o_ready, 1)
                for t, k in steps_beside(n, True):
                    after(t, k)
            oB_evacuate(NU - 1)
            dve.wait_ge(oB_out, 4 * T)
            v.tensor_copy(sub[:, 0:1], sub[:, 4:5]).then_inc(o_ready, 1)
            for t, k in TAIL[:-1]:
                after(t, k)
            link(v.memset(tab_base[:, 0:E], 0.0))
            link(v.tensor_copy(tab_e[:, 0:E], K[:, K_E32:K_E32 + E]))
            v.memset(y_sb[0:SLOTS, :], 0.0).then_inc(zero_ready, 1)
            for k in (6, 7, 8):
                after(T - 1, k)

            def mark_slots(b, e):
                if not isinstance(b, int) or b > 0:
                    dve.wait_ge(slot_done, b)
                bc = slice(b, b + 1) if isinstance(b, int) else bass.ds(b, 1)
                ec = slice(e, e + 1) if isinstance(e, int) else bass.ds(e, 1)
                v.tensor_scalar(slot_b[:, :], K[:, K_SLOT:K_SLOT + SLOTS], tab_base[:, bc], None, ALU.add).then_inc(idx_step, 1)
                v.tensor_copy(Rcur[:, :, :], R[:, :, ec, :].rearrange("p t a k -> p t (a k)"))
                dve.wait_ge(idx_step, 4 * b + 1)
                v.tensor_tensor(onehot[:, :, :], slot_b[:, :].unsqueeze(1).to_broadcast((P, T, SLOTS)),
                                pos[:, :, ec].to_broadcast((P, T, SLOTS)), ALU.is_equal).then_inc(hot_ready, 1)

            def slot_info(b):
                bc = slice(b, b + 1) if isinstance(b, int) else bass.ds(b, 1)
                dve.wait_ge(slot_done, b + 1)
                if not isinstance(b, int) or b > 0:
                    dve.wait_ge(gathered, 16 * b)
                v.tensor_copy(si[:, 0:6], slot_ps).then_inc(idx_step, 1)
                dve.wait_ge(idx_step, 4 * b + 2)
                v.tensor_reduce(gtab[:, bc], si[:, 3:6], AX.X, ALU.add)
                v.scalar_tensor_tensor(out=si[:, 6:7], in0=si[:, 1:2], scalar=float(P), in1=si[:, 0:1],
                                       op0=ALU.mult, op1=ALU.add).then_inc(idx_step, 1)
                dve.wait_ge(idx_step, 4 * b + 3)
                v.scalar_tensor_tensor(out=si[:, 7:8], in0=si[:, 2:3], scalar=K[0:SLOTS, K_SPARE:K_SPARE + 1], in1=si[:, 6:7],
                                       op0=ALU.mult, op1=ALU.subtract).then_inc(idx_step, 1)
                dve.wait_ge(idx_step, 4 * b + 4)
                v.scalar_tensor_tensor(out=stab[:, bc], in0=si[:, 7:8], scalar=-1.0, in1=K[0:SLOTS, K_SPARE:K_SPARE + 1],
                                       op0=ALU.mult, op1=ALU.add)
                v.tensor_copy(gidx[:, :], si[:, 6:7]).then_inc(gidx_ready, 1)

            def gained(b):
                dve.wait_ge(xr_tr, b + 1)
                dve.wait_ge(slot_done, b + 2)
                if not isinstance(b, int) or b > 0:
                    dve.wait_ge(gate_used, C * b)
                    dve.wait_ge(xu_ready, b)
                v.tensor_tensor(xg[:, 0:4, :], xt_ps[0], g2[:, 0:4].unsqueeze(2).to_broadcast((P, 4, SLOTS)), ALU.mult)
                v.tensor_tensor(xg[:, 4:8, :], xt_ps[1], g2[:, 4:8].unsqueeze(2).to_broadcast((P, 4, SLOTS)),
                                ALU.mult).then_inc(xg_ready, 1)

            def gates(b, e):
                ec = slice(e, e + 1) if isinstance(e, int) else bass.ds(e, 1)
                if isinstance(b, int) and b == 0:
                    dve.wait_ge(bias_in, 16)
                    dve.wait_ge(h2_stored, 16 * T)
                v.tensor_copy(bgc[:, :].unsqueeze(2), bgate[:, :, ec]).then_inc(g_step, 1)
                v.tensor_copy(buc[:, :].unsqueeze(2), bup[:, :, ec]).then_inc(g_step, 1)
                dve.wait_ge(g_step, 2 * b + 2)
                dve.wait_ge(gate_used, C * (b + 1))
                if not isinstance(b, int) or b > 0:
                    dve.wait_ge(mid_ready, b)
                for i in range(2):
                    last = v.tensor_tensor(gact[:, 4 * i:4 * i + 4, :], gate_ps[i],
                                           bgc[:, 4 * i:4 * i + 4].unsqueeze(2).to_broadcast((P, 4, SLOTS)), ALU.add)
                last.then_inc(g_read, 1)
                dve.wait_ge(g_read, b + 1)
                v.tensor_scalar(gact, gact, LIMIT, None, ALU.min).then_inc(g_ready, 1)

            def middle(b):
                dve.wait_ge(up_used, C * (b + 1))
                for i in range(2):
                    last = v.tensor_tensor(uact[:, 4 * i:4 * i + 4, :], up_ps[i],
                                           buc[:, 4 * i:4 * i + 4].unsqueeze(2).to_broadcast((P, 4, SLOTS)), ALU.add)
                last.then_inc(u_read, 1)
                dve.wait_ge(u_read, b + 1)
                v.tensor_scalar(uact, uact, LIMIT, -LIMIT, ALU.min, ALU.max).then_inc(u_step, 1)
                dve.wait_ge(u_step, 2 * b + 1)
                dve.wait_ge(g_ready, b + 1)
                v.scalar_tensor_tensor(out=uact, in0=uact, scalar=1.0, in1=gact, op0=ALU.add, op1=ALU.mult).then_inc(u_step, 1)
                dve.wait_ge(u_step, 2 * b + 2)
                dve.wait_ge(sig_ready, b + 1)
                if not isinstance(b, int) or b > 0:
                    dve.wait_ge(mid_hi_ready, b)
                v.tensor_tensor(mid, uact, sig, ALU.mult).then_inc(mid_ready, 1)

            def mid_low(b):
                dve.wait_ge(mid_hi_ready, b + 1)
                v.tensor_tensor(mid_lo[:, :, :], mid, mid_hi[:, :, :].bitcast(F32), ALU.subtract).then_inc(mid_lo_ready, 1)

            def low_parts(b, u0, u1):
                for u in range(u0, u1):
                    c, h = divmod(u, 2)
                    dve.wait_ge(hi_ready, UNITS * b + u + 1)
                    v.tensor_tensor(w_lo[:, u % RING, :], wd[:, c, h * HALF:(h + 1) * HALF],
                                    w_hi[:, u % RING, :].bitcast(F32), ALU.subtract).then_inc(lo_ready, 1)

            def now(b):
                bc = slice(b, b + 1) if isinstance(b, int) else bass.ds(b, 1)
                if not isinstance(b, int) or b > 0:
                    dve.wait_ge(scattered, 16 * b)
                v.tensor_copy(gnow[:, :], gtab[:, bc])
                v.tensor_copy(sidx[:, :], stab[:, bc]).then_inc(now_ready, 1)

            dve.wait_ge(pos_ready, T)
            mark_slots(0, 0)
            slot_info(0)
            mark_slots(1, 1)
            dve.wait_ge(cnt_done, 1)
            link(v.tensor_copy(cnt[:, 0:1], bank[4][0:E, 0:1]))
            link(v.tensor_tensor(cnt[:, 1:1 + NTHR], K[0:E, K_THR:K_THR + NTHR], cnt[:, 0:1].to_broadcast((E, NTHR)), ALU.is_lt))
            link(v.tensor_reduce(cnt[:, 8:9], cnt[:, 1:1 + NTHR], AX.X, ALU.add))
            v.tensor_scalar(nbc[:, :], K[0:E, K_ONE:K_ONE + P], cnt[:, 8:9], None, ALU.mult).then_inc(nbc_ready, 1)
            gained(0)
            slot_info(1)
            for k in (10, 11):
                after(T - 1, k)
            mark_slots(2, 2)
            dve.wait_ge(cum_done, 1)
            link(v.tensor_copy(cum[:, :], bank[4][:, 0:2 * E]))
            link(v.tensor_tensor(le[:, :, :], cum[:, 0:E].unsqueeze(1).to_broadcast((P, NX, E)),
                                 K[:, K_BIDX:K_BIDX + NX].unsqueeze(2).to_broadcast((P, NX, E)), ALU.is_le))
            v.tensor_copy(btab[:, 3, :], le[:, :, E - 1])
            link(v.tensor_reduce(btab[:, 0, :], le[:, :, :], AX.X, ALU.add))
            link(v.tensor_scalar(tab_e[:, E:NB], btab[:, 0, :], float(E - 1), None, ALU.min))
            link(v.tensor_copy(tab_ei[:, :], tab_e[:, :]))
            link(v.tensor_tensor(le[:, :, :], le[:, :, :], cum[:, E:2 * E].unsqueeze(1).to_broadcast((P, NX, E)), ALU.mult))
            link(v.tensor_reduce(btab[:, 1, :], le[:, :, :], AX.X, ALU.add))
            link(v.tensor_tensor(btab[:, 2, :], K[:, K_BIDX:K_BIDX + NX], btab[:, 1, :], ALU.subtract))
            link(v.tensor_scalar(btab[:, 2, :], btab[:, 2, :], 1.0, float(SLOTS), ALU.add, ALU.mult))
            link(v.scalar_tensor_tensor(out=tab_base[:, E:NB], in0=btab[:, 3, :], scalar=2 * FAR, in1=btab[:, 2, :],
                                        op0=ALU.mult, op1=ALU.add))
            v.tensor_copy(further[:, :], cum[:, E - 1:E]).then_inc(table_ready, 1)
            dve.wait_ge(table_ready, 1)
            gates(0, 0)
            gained(1)
            slot_info(2)
            middle(0)
            now(0)
            mid_low(0)
            low_parts(0, 0, RING)
            n_blocks = dve.value_load(further[0:1, 0:1], min_val=0, max_val=OVER) + E
            with dve.Fori(0, n_blocks - 1) as i:
                e_next = dve.value_load(tab_ei[0:1, bass.ds(i + 1, 1)], min_val=0, max_val=E - 1)
                e_look = dve.value_load(tab_ei[0:1, bass.ds(i + 3, 1)], min_val=0, max_val=E - 1)
                mark_slots(i + 3, e_look)
                low_parts(i, RING, UNITS)
                gates(i + 1, e_next)
                gained(i + 2)
                slot_info(i + 3)
                middle(i + 1)
                now(i + 1)
                mid_low(i + 1)
                low_parts(i + 1, 0, RING)
            low_parts(n_blocks - 1, RING, UNITS)

        @block.gpsimd
        def _(pool):
            asked = [0]

            def root(a, n):
                asked[0] += 1
                pool.wait_ge(mean_ready, asked[0])
                half = K[:, K_HALF:K_HALF + 1]
                nc.gpsimd.tensor_tensor(a, a, half if n == 1 else half.to_broadcast((P, n)), ALU.pow).then_inc(root_ready, 1)

            pool.wait_ge(K_in, 16)
            root(st[:, 4:8], T)
            for t in range(T):
                root(rsq[:, :], NQK)
            root(sub[:, 4:8], 4)
            for t in range(T):
                root(st[:, 20 + t:21 + t], 1)
                pool.wait_ge(h2_ready, t + 1)
                pool.dma_start(h2_dram[t * P:(t + 1) * P, :], o_nat[:, t, :]).then_inc(h2_stored, 16)
                if t + 1 < T:
                    root(sub[:, 4:8], 4)
                if t:
                    pool.wait_ge(acc_ready, 2 * t)
                    pool.dma_start(out[(t - 1) * P:t * P, :], xres[:, t - 1, :]).then_inc(acc_stored, 16)
            pool.wait_ge(zero_ready, 1)
            pool.dma_start(out[SEQ:ROWS, :], y_sb[0:SLOTS, :]).then_inc(acc_stored, 16)
            def gather(b):
                pool.wait_ge(gidx_ready, b + 1)
                if not isinstance(b, int) or b > 0:
                    pool.wait_ge(xr_tr, b)
                pool.sem_inc(pool_turn, 1)
                pool.wait_ge(h2_stored, 16 * T)
                nc.gpsimd.indirect_dma_start(
                    out=xrow[0:SLOTS, :], out_offset=None, in_=h2_dram,
                    in_offset=bass.IndirectOffsetOnAxis(ap=gidx[:, 0:1], axis=0)).then_inc(gathered, 16)

            def scatter(b):
                pool.wait_ge(y_ready, b + 1)
                if not isinstance(b, int) or b > 0:
                    pool.wait_ge(scattered, 16 * b)
                pool.sem_inc(pool_turn, 1)
                pool.wait_ge(acc_stored, 16 * (T + 1))
                nc.gpsimd.indirect_dma_start(
                    out=out, out_offset=bass.IndirectOffsetOnAxis(ap=sidx[:, 0:1], axis=0), in_=y_sb[0:SLOTS, :],
                    in_offset=None, compute_op=ALU.add).then_inc(scattered, 16)

            gather(0)
            gather(1)
            pool.wait_ge(acc_ready, 2 * T)
            pool.dma_start(out[(T - 1) * P:T * P, :], xres[:, T - 1, :]).then_inc(acc_stored, 16)
            gather(2)
            pool.wait_ge(table_ready, 1)
            n_blocks = pool.value_load(further[0:1, 0:1], min_val=0, max_val=OVER) + E
            with pool.Fori(0, n_blocks - 1) as i:
                gather(i + 3)
                scatter(i)
            scatter(n_blocks - 1)
            pool.wait_ge(scattered, 16 * n_blocks)
            pool.wait_ge(gathered, 16 * (n_blocks + 2))


def kernel(x, norm1_g, w_in, a_qnorm_g, a_knorm_g, a_lq1, a_lk1, a_lq2, a_lk2, a_subln_g, b_qnorm_g, b_knorm_g,
           w_out, norm2_g, router_w, router_b, w_gate, b_gate, w_up, b_up, w_down, b_down):
    import concourse.bacc as _bacc
    from concourse.bass_utils import run_bass_kernel_spmd as _run

    nc = _bacc.Bacc("TRN2", target_bir_lowering=False, num_devices=1)

    def per_partition(a):
        a = np.asarray(a)[0]
        return np.moveaxis(a.reshape(-1, C, P), 2, 0).transpose(0, 2, 1).reshape(P, -1)

    k, rope = shape_constants()
    arrays = {
        "x": np.asarray(x)[0], "w_in": np.asarray(w_in)[0], "w_out": np.asarray(w_out)[0],
        "w_gate": np.asarray(w_gate)[0], "w_up": np.asarray(w_up)[0], "w_down": np.asarray(w_down)[0],
        "b_down": np.asarray(b_down)[0], "router_b": np.asarray(router_b),
        "consts": k, "rope": rope,
        "cols": np.concatenate([per_partition(norm1_g), per_partition(norm2_g),
                                np.asarray(router_w)[0].reshape(C, P, E).transpose(1, 0, 2).reshape(P, C * E)], axis=1),
        "bias": np.concatenate([per_partition(b_gate), per_partition(b_up)], axis=1),
        "vecs": np.concatenate([np.asarray(a) for a in (a_qnorm_g, a_knorm_g, b_qnorm_g, b_knorm_g, a_lq1, a_lk1,
                                                        a_lq2, a_lk2, a_subln_g)], axis=1),
    }
    arrays = {f"in_{n}": np.ascontiguousarray(a) for n, a in arrays.items()}
    aps = [nc.dram_tensor(n, a.shape, mybir.dt.from_np(a.dtype), kind="ExternalInput").ap() for n, a in arrays.items()]
    out = nc.dram_tensor("out_rows", (ROWS, D), F32, kind="ExternalOutput").ap()
    h2_rows = nc.dram_tensor("h2_rows", (SEQ, D), F32, kind="Internal").ap()
    (x_, w_in_, w_out_, wg_, wu_, wd_, bd_, rb_, k_, rope_, cols_, bias_, vecs_) = aps
    encoder_layer(nc, x_, w_in_, w_out_, wg_, wu_, wd_, bd_, rb_, k_, rope_, cols_, bias_, vecs_, out, h2_rows)
    got = _run(nc, [arrays], core_ids=[0]).results[0]["out_rows"]
    return got[:SEQ].reshape(1, SEQ, D)
```
